# Optimizing a Trainium2 kernel written in Bass

```python
import jax, jax.numpy as jnp
from jax import lax
import numpy as np

D_MODEL = 2048
BATCH = 1
SEQ = 256
DEPTH = 2
DEC_BATCH = 8
DEC_SEQ = 16
PAST_LEN = 128

CHUNK = 64
N_EVEN = (DEPTH + 1) // 2
N_ODD = DEPTH // 2
EPS = 1e-6
A_HEADS = 4
A_WIDTH = D_MODEL
A_HEAD_DIM = A_WIDTH // A_HEADS
GMLP_CHUNK = 128
B_HEADS = 8
B_DK = D_MODEL // B_HEADS
B_DV = D_MODEL // B_HEADS
B_WIDTH = B_HEADS * B_DV
ROPE_BASE = 10000.0
C_HEADS = 8
C_DK = D_MODEL // C_HEADS
C_DV = 2 * C_DK
C_WIDTH = C_HEADS * C_DV
GLA_RANK = 16
GLA_GATE_NORM = 16.0
GLA_BLOCK = 16
E_SPLITS = [A_WIDTH, A_WIDTH, A_WIDTH, B_HEADS * B_DK, B_HEADS * B_DK, B_WIDTH, B_WIDTH]
E_IN = sum(E_SPLITS)
E_MIX = A_WIDTH + B_WIDTH
O_SPLITS = [C_HEADS * C_DK, C_HEADS * C_DK, C_WIDTH, C_WIDTH, GLA_RANK]
O_IN = sum(O_SPLITS)
O_MIX = C_WIDTH

kernel_name = 'streaming_gmlp_retnet_gla_adaln'

def rms_norm(x, g):
    xf = x.astype(jnp.float32)
    y = xf * lax.rsqrt(jnp.mean(xf * xf, axis=-1, keepdims=True) + EPS)
    return (y * g.astype(jnp.float32)).astype(x.dtype)

def head_layer_norm(x, g):
    xf = x.astype(jnp.float32)
    mu = jnp.mean(xf, axis=-1, keepdims=True)
    xc = xf - mu
    var = jnp.mean(xc * xc, axis=-1, keepdims=True)
    return (xc * lax.rsqrt(var + EPS) * g.astype(jnp.float32)).astype(x.dtype)

def rotary(x, pos):
    half = x.shape[-1] // 2
    freqs = ROPE_BASE ** (-jnp.arange(half, dtype=jnp.float32) / half)
    ang = pos.astype(jnp.float32)[:, None] * freqs[None, :]
    cos = jnp.cos(ang)[None, :, None, :]
    sin = jnp.sin(ang)[None, :, None, :]
    xf = x.astype(jnp.float32)
    x1, x2 = xf[..., :half], xf[..., half:]
    return jnp.concatenate([x1 * cos - x2 * sin, x1 * sin + x2 * cos], axis=-1).astype(x.dtype)

def run_blocks(block_fn, S0, xs, block):
    B, H, L = xs[0].shape[:3]
    nb = L // block
    xs_b = tuple(jnp.moveaxis(a.reshape(B, H, nb, block, a.shape[-1]), 2, 0) for a in xs)
    S, o = lax.scan(block_fn, S0, xs_b)
    o = jnp.moveaxis(o, 0, 2).reshape(B, H, L, o.shape[-1])
    return o, S

def retention_block(S, inputs):
    q, k, v = inputs
    L = q.shape[2]
    log_g = jnp.log1p(-jnp.exp2(-5.0 - jnp.arange(B_HEADS, dtype=jnp.float32)))
    t = jnp.arange(L, dtype=jnp.float32)
    diff = t[:, None] - t[None, :]
    decay = jnp.where(diff >= 0, jnp.exp(jnp.maximum(diff, 0.0)[None] * log_g[:, None, None]), 0.0).astype(v.dtype)
    q_dec = jnp.exp((t[None, :] + 1.0) * log_g[:, None]).astype(v.dtype)
    k_dec = jnp.exp((L - 1.0 - t[None, :]) * log_g[:, None]).astype(v.dtype)
    s_dec = jnp.exp(L * log_g).astype(S.dtype)
    scores = jnp.einsum('bhtd,bhsd->bhts', q, k) * decay
    o = (jnp.einsum('bhts,bhsv->bhtv', scores, v)
         + jnp.einsum('bhtd,bhdv->bhtv', q * q_dec[None, :, :, None], S.astype(v.dtype)))
    S_new = s_dec[None, :, None, None] * S + jnp.einsum('bhsd,bhsv->bhdv', k * k_dec[None, :, :, None], v).astype(S.dtype)
    return S_new.astype(S.dtype), o

def gla_block(S, inputs):
    q, k, v, gk = inputs
    L = q.shape[2]
    b = jnp.cumsum(gk, axis=2)
    b_end = b[:, :, -1:, :]
    qf = q.astype(jnp.float32) * jnp.exp(b)
    kf = k.astype(jnp.float32) * jnp.exp(-b)
    causal = jnp.tril(jnp.ones((L, L), dtype=bool))
    scores = jnp.where(causal, jnp.einsum('bhtd,bhsd->bhts', qf, kf), 0.0).astype(v.dtype)
    o = (jnp.einsum('bhts,bhsv->bhtv', scores, v)
         + jnp.einsum('bhtd,bhdv->bhtv', qf.astype(v.dtype), S.astype(v.dtype)))
    k_tail = (k.astype(jnp.float32) * jnp.exp(b_end - b)).astype(v.dtype)
    S_new = (jnp.exp(b_end[:, :, 0, :, None]).astype(S.dtype) * S
             + jnp.einsum('bhsd,bhsv->bhdv', k_tail, v).astype(S.dtype))
    return S_new.astype(S.dtype), o

def spatial_gating(u, v, w_s, b_s):
    B, L = v.shape[:2]
    seg = min(L, GMLP_CHUNK)
    nc = L // seg
    p = jnp.arange(seg)
    mask = (p[None, :] // CHUNK) <= (p[:, None] // CHUNK)
    w = jnp.where(mask[None], w_s[:, :seg, :seg], 0.0).astype(v.dtype)
    vc = v.reshape(B, nc, seg, A_HEADS, A_HEAD_DIM)
    mixed = jnp.einsum('hts,bcshd->bcthd', w, vc) + b_s[:, :seg].T[None, None, :, :, None].astype(v.dtype)
    return u * mixed.reshape(B, L, A_HEADS, A_HEAD_DIM)

def modulate(x, c, norm_g, w_mod, b_mod):
    mod = jax.nn.silu(c) @ w_mod + b_mod
    shift, scale, gate = jnp.split(mod, 3, axis=-1)
    h = rms_norm(x, norm_g) * (1 + scale[:, None, :]) + shift[:, None, :]
    return h, gate[:, None, :]

def even_mixer(h, pos, S0, block, w_in, ln_g, w_s, b_s, ret_g, w_out):
    B, L, _ = h.shape
    proj = h @ w_in
    u, va, za, q, k, vb, zb = jnp.split(proj, np.cumsum(E_SPLITS)[:-1].tolist(), axis=-1)
    u = jax.nn.gelu(u).reshape(B, L, A_HEADS, A_HEAD_DIM)
    va = head_layer_norm(jax.nn.gelu(va).reshape(B, L, A_HEADS, A_HEAD_DIM), ln_g.reshape(A_HEADS, A_HEAD_DIM))
    ya = spatial_gating(u, va, w_s, b_s).reshape(B, L, A_WIDTH) * jax.nn.silu(za)
    q = rotary(q.reshape(B, L, B_HEADS, B_DK), pos).transpose(0, 2, 1, 3)
    k = (rotary(k.reshape(B, L, B_HEADS, B_DK), pos) * (B_DK ** -0.5)).transpose(0, 2, 1, 3)
    vb = vb.reshape(B, L, B_HEADS, B_DV).transpose(0, 2, 1, 3)
    o, S = run_blocks(retention_block, S0, (q, k, vb), block)
    yb = rms_norm(o.transpose(0, 2, 1, 3), ret_g).reshape(B, L, B_WIDTH) * jax.nn.silu(zb)
    y = jnp.concatenate([ya, yb], axis=-1) @ w_out
    return y, S, va.reshape(B, L, A_WIDTH)

def odd_mixer(h, S0, block, w_in, w_gk2, b_gk, gla_g, w_out):
    B, L, _ = h.shape
    proj = h @ w_in
    q, k, v, z, lr = jnp.split(proj, np.cumsum(O_SPLITS)[:-1].tolist(), axis=-1)
    gk = jax.nn.log_sigmoid((lr @ w_gk2 + b_gk).astype(jnp.float32)) / GLA_GATE_NORM
    tr = lambda a, d: a.reshape(B, L, C_HEADS, d).transpose(0, 2, 1, 3)
    q = tr(q * (C_DK ** -0.5), C_DK)
    o, S = run_blocks(gla_block, S0, (q, tr(k, C_DK), tr(v, C_DV), tr(gk, C_DK)), block)
    y = rms_norm(o.transpose(0, 2, 1, 3), gla_g).reshape(B, L, C_WIDTH) * jax.nn.silu(z)
    return y @ w_out, S

def trunk(x, c, pos, ret_state, gla_state, ret_blk, gla_blk,
          norm_g, w_mod, b_mod, w_in_e, gmlp_ln_g, gmlp_ws, gmlp_bs, ret_norm_g, w_out_e,
          w_in_o, w_gk2, b_gk, gla_norm_g, w_out_o, final_g):
    ret_new, gla_new, v_rows = [], [], []
    for l in range(DEPTH):
        h, gate = modulate(x, c, norm_g[l], w_mod[l], b_mod[l])
        i = l // 2
        if l % 2 == 0:
            y, S, va = even_mixer(h, pos, ret_state[i], ret_blk, w_in_e[i], gmlp_ln_g[i], gmlp_ws[i],
                                  gmlp_bs[i], ret_norm_g[i], w_out_e[i])
            ret_new.append(S)
            v_rows.append(va)
        else:
            y, S = odd_mixer(h, gla_state[i], gla_blk, w_in_o[i], w_gk2[i], b_gk[i], gla_norm_g[i], w_out_o[i])
            gla_new.append(S)
        x = x + gate * y
    return rms_norm(x, final_g), jnp.stack(ret_new), jnp.stack(gla_new), jnp.stack(v_rows)

def setup_inputs(seed: int = 0) -> dict:
    key = jax.random.key(seed)
    ks = jax.random.split(key, 24)
    f32 = jnp.float32
    nrm = lambda k, shape, s: jax.random.normal(k, shape, f32) * s
    return {
        'x_prompt': nrm(ks[0], (BATCH, SEQ, D_MODEL), 1.0),
        'x_sample': nrm(ks[1], (DEC_BATCH, DEC_SEQ, D_MODEL), 1.0),
        'state_ret': nrm(ks[2], (N_EVEN, DEC_BATCH, B_HEADS, B_DK, B_DV), B_DK ** -0.5),
        'state_gla': nrm(ks[3], (N_ODD, DEC_BATCH, C_HEADS, C_DK, C_DV), C_DK ** -0.5),
        'c_prompt': nrm(ks[4], (BATCH, D_MODEL), 1.0),
        'c_sample': nrm(ks[5], (DEC_BATCH, D_MODEL), 1.0),
        'norm_g': 1.0 + nrm(ks[6], (DEPTH, D_MODEL), 0.02),
        'w_mod': nrm(ks[7], (DEPTH, D_MODEL, 3 * D_MODEL), D_MODEL ** -0.5),
        'b_mod': nrm(ks[8], (DEPTH, 3 * D_MODEL), 0.02),
        'w_in_e': nrm(ks[9], (N_EVEN, D_MODEL, E_IN), D_MODEL ** -0.5),
        'gmlp_ln_g': 1.0 + nrm(ks[10], (N_EVEN, A_WIDTH), 0.02),
        'gmlp_ws': nrm(ks[11], (N_EVEN, A_HEADS, GMLP_CHUNK, GMLP_CHUNK), GMLP_CHUNK ** -0.5),
        'gmlp_bs': 1.0 + nrm(ks[12], (N_EVEN, A_HEADS, GMLP_CHUNK), 0.02),
        'ret_norm_g': 1.0 + nrm(ks[13], (N_EVEN, B_DV), 0.02),
        'w_out_e': nrm(ks[14], (N_EVEN, E_MIX, D_MODEL), E_MIX ** -0.5),
        'w_in_o': nrm(ks[15], (N_ODD, D_MODEL, O_IN), D_MODEL ** -0.5),
        'w_gk2': nrm(ks[16], (N_ODD, GLA_RANK, C_HEADS * C_DK), GLA_RANK ** -0.5),
        'b_gk': nrm(ks[17], (N_ODD, C_HEADS * C_DK), 0.02),
        'gla_norm_g': 1.0 + nrm(ks[18], (N_ODD, C_DV), 0.02),
        'w_out_o': nrm(ks[19], (N_ODD, O_MIX, D_MODEL), O_MIX ** -0.5),
        'final_g': 1.0 + nrm(ks[20], (D_MODEL,), 0.02),
    }

def reference(x_prompt, x_sample, state_ret, state_gla, c_prompt, c_sample,
              norm_g, w_mod, b_mod, w_in_e, gmlp_ln_g, gmlp_ws, gmlp_bs, ret_norm_g, w_out_e,
              w_in_o, w_gk2, b_gk, gla_norm_g, w_out_o, final_g):
    weights = (norm_g, w_mod, b_mod, w_in_e, gmlp_ln_g, gmlp_ws, gmlp_bs, ret_norm_g, w_out_e,
               w_in_o, w_gk2, b_gk, gla_norm_g, w_out_o, final_g)
    bp, lp = x_prompt.shape[:2]
    ls = x_sample.shape[1]
    ret0 = jnp.zeros((N_EVEN, bp, B_HEADS, B_DK, B_DV), x_prompt.dtype)
    gla0 = jnp.zeros((N_ODD, bp, C_HEADS, C_DK, C_DV), x_prompt.dtype)
    y_prompt, ret_prompt, gla_prompt, _ = trunk(x_prompt, c_prompt, jnp.arange(lp), ret0, gla0,
                                                CHUNK, GLA_BLOCK, *weights)
    y_sample, ret_sample, gla_sample, gmlp_v_sample = trunk(x_sample, c_sample, PAST_LEN + jnp.arange(ls),
                                                            state_ret, state_gla, ls, ls, *weights)
    return (y_prompt, y_sample, ret_prompt, ret_sample, gla_prompt, gla_sample, gmlp_v_sample)


_drawn_inputs = setup_inputs


def setup_inputs(seed=0):
    import zlib

    import numpy as np

    out = dict(_drawn_inputs(seed))
    spreads = {}
    factors = {'gmlp_ln_g': 23.303,
     'gmlp_bs': 19.395,
     'ret_norm_g': 27.508,
     'b_gk': 4.852,
     'gla_norm_g': 100.645,
     'final_g': 23.025}
    for name, (base, spread) in spreads.items():
        noise = np.random.default_rng([zlib.crc32(name.encode()), seed]).standard_normal(out[name].shape)
        drawn = base * np.exp(spread * noise) if base else spread * noise
        out[name] = __import__('jax').numpy.asarray(drawn.astype(out[name].dtype))
    for name, factor in factors.items():
        out[name] = (out[name] * factor).astype(out[name].dtype)
    return out
```

```python
from contextlib import ExitStack

import numpy as np

import concourse.bass as bass
from concourse import mybir
from concourse.alu_op_type import AluOpType as ALU

F32 = mybir.dt.float32
F32R = mybir.dt.float32r
U8 = mybir.dt.uint8
ACT = mybir.ActivationFunctionType

P = 128
D = 2048
KT = D // P
NB = 8
LS = 16
NT = 3
NTOK = NT * P
SMP = 2 * P
W = 512
PAST = 128
A_HEADS, B_HEADS, C_HEADS = 4, 8, 8
DK = 256
DVB, DVC = 256, 512
KH = DK // P
RANK = 16
GATE = 1 / 16.0
EPS = 1e-6
NC9 = 1 + NB
LOROW = 64
BROW, GROW = 96, 97
NROW = 98

NSLOT = 4
GK = 2
LEAD = 16
AHEAD = 3
R_MOD = (0, 96)
R_GM, R_RT, R_GL = 24, 56, 120
A_GM, A_RT, A_GL = 0, 20, 44
Y_GM, Y_RT, Y_GL = 0, 16, 32
O_GM, O_RT, O_GL = 0, 8, 16
Z_RT, Z_GL = NT * A_HEADS, NT * (A_HEADS + B_HEADS)
YB = 8
NST = 4
CH_RT, CH_GL = 4, 8
N_RT = CH_RT * B_HEADS

HC_PW, HC_Q, HC_Q2, HC_K, HC_KE, HC_KO, HC_S = 0, 3, 6, 9, 11, 12, 13


def build(nc, a, consts, outs):
    y_p, y_s, ret_p, ret_s, gla_p, gla_s, gmlp_v = outs
    gate_dram = nc.dram_tensor("gate_rows", [2, NC9, D], F32, kind="Internal").ap()

    w_e = a["w_in_e"][0].rearrange("(k p) n -> p k n", p=P)
    w_o = a["w_in_o"][0].rearrange("(k p) n -> p k n", p=P)
    wo = [a["w_out_e"][0].rearrange("(k p) n -> p k n", p=P), a["w_out_o"][0].rearrange("(k p) n -> p k n", p=P)]
    w_m = [a["w_mod"][l].rearrange("(k p) n -> p k n", p=P) for l in range(2)]
    b_m = a["b_mod"]
    v_rows = gmlp_v[0].rearrange("b l d -> (b l) d")
    st_r, st_g = a["state_ret"][0], a["state_gla"][0]

    with ExitStack() as ctx:
        def sb(name, shape, dt=F32):
            return ctx.enter_context(nc.sbuf_tensor(name, shape, dt))

        def bank(name, shape):
            return ctx.enter_context(nc.psum_tensor(name, shape, F32))

        def sem(name):
            return ctx.enter_context(nc.semaphore(name))

        acc = bank("acc", [P, NT, W])
        T = [bank("turn0", [P, W]), bank("turn1", [P, W])]
        SC = bank("scores", [P, W])
        OB = [bank("mixed0", [P, W]), bank("mixed1", [P, W])]

        raw = [sb(f"raw{j}", [P, GK, W]) for j in range(NSLOT)]
        whi = [sb(f"whi{j}", [P, GK, W], F32R) for j in range(NSLOT)]
        wlo = [sb(f"wlo{j}", [P, GK, W], F32R) for j in range(NSLOT)]
        hT = [sb("hT_hi", [P, KT, NTOK], F32R), sb("hT_lo", [P, KT, NTOK], F32R)]
        yT = [sb("yT_hi", [P, YB, NTOK], F32R), sb("yT_lo", [P, YB, NTOK], F32R)]
        x = sb("x", [P, NT, D])
        ident = sb("ident", [P, P])
        sel = sb("sel", [P, 10])
        modT = sb("modT", [P, 2 * KT, 10])
        cTf = sb("cTf", [P, KT, NC9])
        small = sb("small", [P, 32])
        stats = sb("stats", [P, NT, 4, 6])
        cst = sb("cst", [P, 4])
        state = [sb(f"state{s}", [P, 1024]) for s in range(NST)]
        qmask = sb("qmask", [P, KH, NB, 32])
        work = sb("work", [P, 10992])
        neg_half, zero = cst[:, 0:3], cst[:, 3:4]
        mean_var = small[:, 0:6].rearrange("p (t c) -> p t c", c=2)
        sq, ms, rstd, fac = small[:, 8:11], small[:, 12:15], small[:, 16:19], small[:, 20:23]

        def carve(at, *shape):
            v = work[:, at:at + int(np.prod(shape))]
            if len(shape) == 2:
                v = v.rearrange("p (a b) -> p a b", a=shape[0])
            if len(shape) == 3:
                v = v.rearrange("p (a b c) -> p a b c", a=shape[0], b=shape[1])
            return v

        diag = carve(0, NT, P)
        modsb = [carve(512 + W * i, W) for i in range(2)]
        gsb = [carve(1536 + W * i, W) for i in range(2)]
        hf = [carve(2560 + NTOK * i, NTOK) for i in range(2)]
        crow, crow2 = carve(3584, D), carve(5632, D)
        cT = yT[0][:, :, :].rearrange("p a b -> p (a b)")[:, 0:KT * P].rearrange("p (k c) -> p k c", k=KT)
        ws_nat, ws_diag = carve(7680, A_HEADS, P), carve(8192, A_HEADS, P)
        wsT_all = carve(8704, A_HEADS, 2, P)
        bsT = carve(9728, 2, A_HEADS)
        va, ug, wz = carve(0, NT, W), carve(1536, NT, W), carve(3072, NT, W)
        ln_g = carve(4608, W)
        wsT = carve(9744, 2, P)
        bs_cur = carve(10000, 2)
        cs, sn = carve(0, NT, P), carve(384, NT, P)
        mask01 = carve(768, W)
        hc_all, hc = carve(1280, B_HEADS, 16), carve(1408, 16)
        ret_g = carve(1424, DVB)
        qkr = carve(1680, NT, W)
        qkT = carve(3216, 2 * KH, NTOK)
        swp = carve(4752, W)
        sTb = carve(5264, W)
        vb, wb = carve(5776, NT, DVB), carve(6544, NT, DVB)
        onb = carve(7312, NT, DVB)
        kob = carve(8080, DK)
        pst = carve(8336, KH, DVB)
        C0 = 9326
        mask_u = carve(C0, P).bitcast(U8)
        smask = carve(C0 + 128, NTOK)
        gla_g = carve(C0 + 512, W)
        parity = carve(C0 + 1024, 2)
        lrT = carve(C0 + 1026, NTOK)
        wlr_raw, koc = carve(C0 + 1410, KT, RANK), carve(C0 + 1410, DK)
        gkw = carve(0, DK)
        eb, bend = carve(256, KH, NB), carve(272, KH)
        qkTc = carve(276, 2 * KH, NTOK)
        onc = carve(276, NT, W)
        bb = carve(1812, KH, NTOK)
        ktok = carve(1812, NT, DK)
        qd, kd = carve(2580, KH, NTOK), carve(3348, KH, NTOK)
        lev = [carve(4116, KH, 2 * P), carve(4628, KH, 2 * P)]
        pstc = carve(4116, KH, DVC)
        ee = carve(5140, KH, NTOK)
        vc = carve(5908, NT, W)
        wc = [carve(7444, W), carve(7956, W)]
        sTc = carve(8468, W)
        flat = [t[:, :, :].rearrange("p a b -> p (a b)")[:, 0:KT * RANK].rearrange("p (k c) -> p k c", k=KT) for t in yT]
        wlr = flat
        lr_tok = carve(5140, NT, RANK)
        out_tmp = {"gm": carve(5120, NT, W), "rt": carve(3216, NT, W), "gl": carve(2580, NT, W)}
        out_g = {"gm": carve(6656, 2, W), "rt": carve(5776, 2, W), "gl": carve(4116, 2, W)}

        names = """passed hi_ready lo_ready w_used acc_full const_in ws_in bs_in x_in c_in ident_done const_done
            th_done cs_done cTf_full cTf_done cT_done ws_zero ws_masked wsT_full wsT_done
            mod_full modsb_done sel_full sel_done ms_done rstd_done diag_done modT_done
            xT_full h_prompt h_done hT_hi_done hT_done
            ln_in wcur_done va_done va_out mix_full mix_done z_tanh y_done yb_full yb_hi yb_lo g_in x_added
            rt_const rot_done qkT_full qkT_done sc_full sT_done kd_done qm_done v_done o_full o_done
            pst_full pst_done pst_out up_full up_done
            gl_const lrw_in lrw_hi lrw_done lr_full lr_tok_done lrT_full ones_done lrT_done gkw_in gk_full gk_ln
            gk_done dif_done exp_done dec_done lev_used kt_full kt_done fg_in final_done y_out""".split()
        s = {n: sem(n) for n in names}
        raw_in = [sem(f"raw_in{j}") for j in range(NSLOT)]
        acc_out = [sem(f"acc_out{t}") for t in range(NT)]
        rows_in = [sem(f"rows_in{q}") for q in range(2)]
        gate_out = [sem(f"gate_out{q}") for q in range(2)]
        st_in = [sem(f"st_in{i}") for i in range(NST)]
        st_out = [sem(f"st_out{i}") for i in range(NST)]

        def at_least(eng, sm, n):
            if not isinstance(n, int) or n > 0:
                eng.wait_ge(sm, n)

        def acc_ready(eng, t, ai, r):
            if t < 2:
                eng.wait_ge(s["acc_full"], 2 * ai + t + 1)
            else:
                eng.wait_ge(s["w_used"], 4 * r + 4 + LEAD)

        def walk(eng, e):
            e["start"]()
            e["modulation"](0)
            with eng.Fori(0, 2) as ph:
                with eng.Fori(0, 2) as hh:
                    e["gmlp"](ph * 2 + hh, ph * 16 + hh * 6 + R_GM, ph * 10 + hh * 3 + A_GM,
                              ph * 8 + hh * 4 + Y_GM, hh * 4, ph * 4 + O_GM)
                with eng.Fori(0, 4) as pn:
                    e["out"]("gm", pn, ph * 8, ph * 16 + pn + (R_GM + 12), ph * 10 + pn + (A_GM + 6),
                             ph * 8 + (Y_GM + YB), ph * 4 + pn + O_GM, False)
            e["ret_setup"]()
            with eng.Fori(0, 2) as ph:
                with eng.Fori(0, 4) as hh:
                    e["ret"](ph * 4 + hh, ph * 20 + hh * 4 + R_RT, ph * 12 + hh * 2 + A_RT,
                             ph * 8 + hh * 2 + Y_RT, hh * 2, ph * 4 + O_RT)
                with eng.Fori(0, 4) as pn:
                    e["out"]("rt", pn, ph * 8 + 16, ph * 20 + pn + (R_RT + 16), ph * 12 + pn + (A_RT + 8),
                             ph * 8 + (Y_RT + YB), ph * 4 + pn + O_RT, False)
            e["modulation"](1)
            e["gla_setup"]()

            def gla_heads(ph):
                with eng.Fori(0, 2) as hh:
                    e["gla"](hh + ph * 2, hh * 6 + (ph * 16 + R_GL), hh * 3 + (ph * 10 + A_GL),
                             hh * 4 + (ph * 8 + Y_GL), hh * 4, ph * 4 + O_GL)

            def gla_out(ph, pn, last):
                e["out"]("gl", pn, ph * 8, pn + (ph * 16 + R_GL + 12), pn + (ph * 10 + A_GL + 6),
                         ph * 8 + (Y_GL + YB), pn + (ph * 4 + O_GL), last)

            with eng.Fori(0, 3) as ph:
                gla_heads(ph)
                with eng.Fori(0, 4) as pn:
                    gla_out(ph, pn, False)
            gla_heads(3)
            with eng.Fori(0, 3) as pn:
                gla_out(3, pn, False)
            gla_out(3, 3, True)
            e["finish"]()

        def modulation_loops(eng, pair):
            with eng.Fori(0, 2) as kind:
                with eng.Fori(0, 2) as i:
                    pair(kind * 2 + i, i, False)
            for i in range(2):
                pair(i + 4, i, True)

        def nothing(*_):
            pass

        def apart(eng):
            eng.sem_inc(s["passed"], 1)

        def lead(eng, sems):
            for sm in sems:
                eng.sem_inc(sm, LEAD)

        ctx.enter_context(nc.allow_non_contiguous_dma(reason="the offsets of the mixing, a few hundred numbers"))
        block = ctx.enter_context(nc.Block())

        @block.sync
        def _(sp):
            def load(r, j, src):
                at_least(sp, s["lo_ready"], 4 * r + (j - 3))
                if not isinstance(r, int):
                    apart(sp)
                for k in range(GK):
                    dst, part = raw[j][:, k, :], src[:, k]
                    if len(part.shape) == 3:
                        dst = dst.rearrange("p (s n) -> p s n", s=2)
                    sp.dma_start(dst, part).then_inc(raw_in[j], 16)

            def panel(r, src):
                for q in range(2):
                    for j in range(NSLOT):
                        load(r + q, j, src(8 * q + GK * j))

            def start():
                sp.dma_start(crow[0:1, :], a["c_prompt"]).then_inc(s["c_in"], 16)
                sp.dma_start(crow[1:NC9, :], a["c_sample"]).then_inc(s["c_in"], 16)

            def modulation(layer):
                def pair(mh, i, gate):
                    for q in range(2):
                        for half in range(2):
                            for j in range(NSLOT):
                                r = mh * 4 + (R_MOD[layer] + 2 * q + half)
                                k = 8 * half + GK * j
                                load(r, j, w_m[layer][:, k:k + GK, bass.ds(mh * (2 * W) + q * W, W)])
                if layer == 0:
                    first_pair(pair)
                else:
                    modulation_loops(sp, pair)

            def first_pair(pair):
                for q in range(2):
                    for half in range(2):
                        for j in range(NSLOT):
                            load(2 * q + half, j, w_m[0][:, 8 * half + GK * j:8 * half + GK * j + GK, q * W:q * W + W])
                with sp.Fori(1, 6) as mh:
                    pair(mh, 0, False)

            def gmlp(h, r, ai, yi, yb, oi):
                for part, rr in ((1, 0), (0, 2), (2, 4)):
                    panel(r + rr, lambda k: w_e[:, k:k + GK, bass.ds(h * W + part * D, W)])

            def two_projections(w, c0, gap, h):
                def src(k):
                    v = w[:, k:k + GK, c0:c0 + 2 * gap].rearrange("p k (s n) -> p k s n", s=2)
                    return v[:, :, :, bass.ds(h * DK, DK)]
                return src

            def ret(h, r, ai, yi, yb, oi):
                panel(r, two_projections(w_e, 3 * D, D, h))
                panel(r + 2, two_projections(w_e, 5 * D, D, h))

            def gla(h, r, ai, yi, yb, oi):
                panel(r, two_projections(w_o, 0, D, h))
                panel(r + 2, lambda k: w_o[:, k:k + GK, bass.ds(h * W + 2 * D, W)])
                panel(r + 4, lambda k: w_o[:, k:k + GK, bass.ds(h * W + 4 * D, W)])

            def out(kind, pn, kb, r, ai, yi, oi, last):
                layer = int(kind == "gl")
                for j in range(NSLOT):
                    load(r, j, wo[layer][:, bass.ds(kb + GK * j, GK), bass.ds(pn * W, W)])
                sp.wait_ge(s["yb_full"], yi)
                for q in range(2):
                    sp.wait_ge(gate_out[q], 32 * (layer + 1))
                if kind == "gl":
                    sp.wait_ge(s["pst_out"], kb * 4 + (16 * (B_HEADS + 2)))
                sp.wait_ge(acc_out[2], ai + LEAD)
                apart(sp)
                g = out_g[kind]
                sp.dma_start(g[:, 0, :], gate_dram[layer, 0, bass.ds(pn * W, W)].partition_broadcast(P))\
                  .then_inc(s["g_in"], 16)
                sp.dma_start(g[:, 1, :], gate_dram[layer, 1:NC9, bass.ds(pn * W, W)]
                             .rearrange("b (o n) -> b o n", o=1).to_broadcast([NB, LS, W])).then_inc(s["g_in"], 16)

            def finish():
                for t in range(NT):
                    sp.wait_ge(s["final_done"], t + 1)
                    dst = y_s.rearrange("b l d -> (b l) d") if t == 2 else y_p[0, P * t:P * t + P, :]
                    sp.dma_start(dst, x[:, t, :]).then_inc(s["y_out"], 16)
                sp.wait_ge(s["y_out"], 16 * NT)
                sp.wait_ge(s["va_out"], 16 * A_HEADS)
                sp.wait_ge(s["pst_out"], 16 * (B_HEADS + C_HEADS))
                for i in range(NST):
                    sp.wait_ge(st_out[i], 16 * (B_HEADS + 2 * C_HEADS))

            walk(sp, dict(start=start, modulation=modulation, gmlp=gmlp, ret_setup=nothing, ret=ret,
                          gla_setup=nothing, gla=gla, out=out, finish=finish))

        @block.gpsimd
        def _(pool):
            def start():
                lead(pool, [s["x_added"], s["y_done"]])
                pool.dma_start(sel[:, :], consts["sel"]).then_inc(s["const_in"], 16)
                pool.dma_start(ws_nat, a["gmlp_ws"][0].rearrange("h t s -> t h s")).then_inc(s["ws_in"], 16)
                pool.memset(cst[:, 0:3], -0.5)
                pool.memset(cst[:, 3:4], 0.0)
                pool.memset(qmask[:, :, :, :], 0.0)
                pool.memset(ws_diag, 0.0).then_inc(s["ws_zero"], 1)
                pool.memset(ident[:, :], 0.0)
                pool.drain()
                pool.affine_select(out=ident[:, :], in_=ident[:, :], compare_op=ALU.not_equal, fill=1.0, base=0,
                                   pattern=[[-1, P]], channel_multiplier=1).then_inc(s["ident_done"], 1)
                pool.wait_ge(s["ws_zero"], 1)
                for b in range(NB):
                    pool.dma_start(ws_diag[LS * b:LS * b + LS, :, LS * b:LS * b + LS],
                                   a["gmlp_ws"][0, :, 0:LS, 0:LS].rearrange("h t s -> t h s")).then_inc(s["ws_in"], 16)
                    pool.dma_start(bsT[LS * b:LS * b + LS, 1, :],
                                   a["gmlp_bs"][0, :, 0:LS].rearrange("h t -> t h")).then_inc(s["bs_in"], 16)
                pool.dma_start(bsT[:, 0, :], a["gmlp_bs"][0].rearrange("h t -> t h")).then_inc(s["bs_in"], 16)
                pool.dma_start(x[:, 0:2, :], a["x_prompt"][0].rearrange("(t p) d -> p t d", p=P)).then_inc(s["x_in"], 16)
                pool.dma_start(x[:, 2, :], a["x_sample"].rearrange("b l d -> (b l) d")).then_inc(s["x_in"], 16)

            def rsqrt(n):
                pool.wait_ge(s["ms_done"], n)
                pool.tensor_tensor(rstd, ms, neg_half, ALU.pow).then_inc(s["rstd_done"], 1)

            def modulation(layer):
                rsqrt(1 if layer == 0 else N_NORM_1)

                def pair(mh, i, gate):
                    for q in range(2):
                        at_least(pool, s["sel_full"], mh * 2 + (12 * layer + q - 1) + LEAD)
                        apart(pool)
                        pool.dma_start(modsb[q][BROW:BROW + 1, :], b_m[layer:layer + 1, bass.ds(mh * (2 * W) + q * W, W)])\
                            .then_inc(rows_in[q], 16)
                        pool.dma_start(modsb[q][GROW:GROW + 1, :],
                                       a["norm_g"][layer:layer + 1, bass.ds(i * (2 * W) + q * W, W)])\
                            .then_inc(rows_in[q], 16)
                    if gate:
                        for q in range(2):
                            pool.wait_ge(s["sel_done"], mh * 2 + (12 * layer + q + 1) + LEAD)
                            apart(pool)
                            pool.dma_start(gate_dram[layer, :, bass.ds(i * (2 * W) + q * W, W)], gsb[q][0:NC9, :])\
                                .then_inc(gate_out[q], 16)
                modulation_loops(pool, pair)

            def products(ai, z0, y, gate_tile):
                for t in range(NT):
                    pool.wait_ge(acc_out[t], ai + LEAD)
                    pool.tensor_tensor(y[:, t, :], y[:, t, :], gate_tile(t), ALU.mult).then_inc(s["y_done"], 1)

            def gmlp(h, r, ai, yi, yb, oi):
                at_least(pool, s["va_done"], h * NT + LEAD)
                apart(pool)
                pool.dma_start(ln_g, a["gmlp_ln_g"][0, bass.ds(h * W, W)].partition_broadcast(P)).then_inc(s["ln_in"], 16)
                rsqrt(h + 2)
                pool.wait_ge(s["va_done"], h * NT + NT + LEAD)
                apart(pool)
                pool.dma_start(v_rows[:, bass.ds(h * W, W)], va[:, 2, :]).then_inc(s["va_out"], 16)
                pool.wait_ge(s["mix_done"], h * NT + NT + LEAD)
                products(ai + 3, h * NT, ug, lambda t: wz[:, t, :])

            def out(kind, pn, kb, r, ai, yi, oi, last):
                for t in range(NT):
                    pool.wait_ge(acc_out[t], ai + 1 + LEAD)
                    xs = x[:, t, bass.ds(pn * W, W)]
                    pool.tensor_tensor(xs, xs, out_tmp[kind][:, t, :], ALU.add).then_inc(s["x_added"], 1)

            def ret_setup():
                pool.wait_ge(s["x_added"], NT * O_RT + LEAD)
                for dst, src in ((cs, consts["cos"]), (sn, consts["sin"]), (mask01, consts["mask01"]),
                                 (hc_all, consts["hc"]), (ret_g, a["ret_norm_g"][0].partition_broadcast(P))):
                    pool.dma_start(dst, src).then_inc(s["rt_const"], 16)
                for dst, src in ((smask, consts["scan_mask"]), (parity, consts["parity"]),
                                 (gla_g, a["gla_norm_g"][0].partition_broadcast(P))):
                    pool.dma_start(dst, src).then_inc(s["gl_const"], 16)
                pool.dma_start(wlr_raw, w_o[:, :, 12288:12288 + RANK]).then_inc(s["lrw_in"], 16)

            def ret_piece(st, h, c):
                return st[4 * (c % 2):4 * (c % 2) + 4, bass.ds(h, 1),
                          P * (c // 2):P * (c // 2) + P, :].rearrange("b o p v -> p (b o) v")

            def gla_piece(st, h, c):
                return st[2 * (c % 4):2 * (c % 4) + 2, bass.ds(h, 1),
                          P * (c // 4):P * (c // 4) + P, :].rearrange("b o p v -> p (b o) v")

            def st_free(uses):
                for c in range(NST):
                    pool.wait_ge(st_out[c], uses * 16)

            def st_load(piece, src, h, c, n):
                pool.dma_start(state[c % NST][:, :].rearrange("p (b v) -> p b v", b=n), piece(src, h, c))\
                    .then_inc(st_in[c % NST], 16)

            def st_store(piece, dst, h, c, sc, n):
                pool.wait_ge(s["up_done"], sc * 2 + 2)
                apart(pool)
                pool.dma_start(piece(dst, h, c), state[c % NST][:, :].rearrange("p (b v) -> p b v", b=n))\
                    .then_inc(st_out[c % NST], 16)

            def spread_q(q_samples, n):
                for b2 in range(2):
                    qv = q_samples.rearrange("p k (b c l) -> p k b c l", c=2, l=LS)[:, :, :, b2, :]
                    dst = qmask[:, :, :, :].rearrange("p k (b c) l -> p k b c l", c=2)[:, :, :, b2, LS * b2:LS * b2 + LS]
                    for kt in range(KH):
                        last = pool.tensor_copy(dst[:, kt], qv[:, kt])
                last.then_inc(s["qm_done"], 1)

            def ret(h, r, ai, yi, yb, oi):
                for c in range(CH_RT):
                    st_load(ret_piece, st_r, h, c, 4)
                pool.wait_ge(s["qkT_done"], h * NT + NT)
                apart(pool)
                spread_q(qkT[:, 0:KH, SMP:NTOK], h)
                pool.wait_ge(s["pst_done"], h + 1)
                apart(pool)
                pool.dma_start(ret_p[0, 0, bass.ds(h, 1)].rearrange("o (k p) v -> p (o k) v", p=P), pst)\
                    .then_inc(s["pst_out"], 16)
                for c in range(CH_RT):
                    st_store(ret_piece, ret_s[0], h, c, h * CH_RT + c, 4)
                rsqrt(h + (2 + A_HEADS))
                pool.wait_ge(s["o_done"], h * NT + NT + LEAD)
                products(ai + 2, 0, onb, lambda t: wb[:, t, :])
                st_free(h + 1)

            def gla_setup():
                pool.wait_ge(s["hT_done"], 2 * KT)
                pool.memset(lrT[0:32, :], 1.0).then_inc(s["ones_done"], 1)

            def gla(h, r, ai, yi, yb, oi):
                for c in range(NST):
                    st_load(gla_piece, st_g, h, c, 2)
                at_least(pool, s["gk_full"], h * KH + LEAD)
                apart(pool)
                pool.dma_start(gkw[0:RANK, :], a["w_gk2"][0, :, bass.ds(h * DK, DK)]).then_inc(s["gkw_in"], 16)
                pool.dma_start(gkw[RANK:RANK + 1, :], a["b_gk"][:, bass.ds(h * DK, DK)]).then_inc(s["gkw_in"], 16)
                pool.wait_ge(s["dec_done"], h * 5 + 1)
                apart(pool)
                spread_q(qd[:, :, SMP:NTOK], h)
                pool.wait_ge(s["pst_done"], h * KH + (B_HEADS + KH))
                apart(pool)
                pool.dma_start(gla_p[0, 0, bass.ds(h, 1)].rearrange("o (k p) v -> p (o k) v", p=P), pstc)\
                    .then_inc(s["pst_out"], 16)
                for c in range(CH_GL):
                    st_store(gla_piece, gla_s[0], h, c, h * CH_GL + (N_RT + c), 2)
                    if 1 <= c <= NST:
                        pool.wait_ge(st_out[c - 1], h * 32 + 16 * (B_HEADS + 1))
                        apart(pool)
                        st_load(gla_piece, st_g, h, c - 1 + NST, 2)
                rsqrt(h + (3 + A_HEADS + B_HEADS))
                pool.wait_ge(s["o_done"], h * NT + (B_HEADS + 1) * NT + LEAD)
                products(ai + 3, 0, onc, lambda t: wc[t % 2])
                st_free(h * 2 + (B_HEADS + 2))

            def finish():
                pool.wait_ge(s["x_added"], NT * 32 + LEAD)
                apart(pool)
                pool.dma_start(work[:, 0:D], a["final_g"].partition_broadcast(P)).then_inc(s["fg_in"], 16)
                rsqrt(4 + A_HEADS + B_HEADS + C_HEADS - 1)

            N_NORM_1 = 2 + A_HEADS + B_HEADS
            walk(pool, dict(start=start, modulation=modulation, gmlp=gmlp, ret_setup=ret_setup, ret=ret,
                            gla_setup=gla_setup, gla=gla, out=out, finish=finish))

        @block.scalar
        def _(act):
            def split(r, j):
                jj, rr = (j + AHEAD) % NSLOT, r + (j + AHEAD) // NSLOT
                act.wait_ge(raw_in[jj], 32 * rr + 32)
                at_least(act, s["w_used"], 4 * r + j + LEAD)
                act.activation(whi[jj][:, :, :], raw[jj][:, :, :], ACT.Copy).then_inc(s["hi_ready"], 1)

            def splits(r):
                for j in range(NSLOT):
                    split(r, j)

            def start():
                lead(act, [s["modsb_done"]])
                act.wait_ge(s["c_in"], 32)
                act.activation(crow2[0:NC9, :], crow[0:NC9, :], ACT.Tanh, scale=0.5).then_inc(s["th_done"], 1)
                for j in range(AHEAD):
                    act.wait_ge(raw_in[j], 32)
                    act.activation(whi[j][:, :, :], raw[j][:, :, :], ACT.Copy).then_inc(s["hi_ready"], 1)
                for i in range(2):
                    act.wait_ge(s["wsT_full"], i + 1)
                    act.activation(wsT_all[:, :, i, :], OB[i][:, :].rearrange("p (h t) -> p h t", h=A_HEADS),
                                   ACT.Copy).then_inc(s["wsT_done"], 1)
                act.wait_ge(s["cTf_full"], 1)
                act.activation(cTf[:, :, :], SC[:, 0:KT * NC9].rearrange("p (k c) -> p k c", k=KT), ACT.Copy,
                               scale=0.5).then_inc(s["cTf_done"], 1)

            def modulation(layer):
                if layer:
                    act.wait_ge(s["x_added"], NT * O_GL + LEAD)

                def pair(mh, i, gate):
                    for q in range(2):
                        for half in range(2):
                            splits(mh * 4 + (R_MOD[layer] + 2 * q + half))
                    for q in range(2):
                        m = mh * 2 + (12 * layer + q)
                        act.wait_ge(s["mod_full"], m + 1)
                        act.activation(modsb[q][0:BROW, :], T[q][0:BROW, :], ACT.Copy).then_inc(s["modsb_done"], 1)
                    if gate:
                        for q in range(2):
                            act.wait_ge(s["sel_full"], mh * 2 + (12 * layer + q + 1) + LEAD)
                            at_least(act, gate_out[q], i * 16 + 32 * layer)
                            act.activation(gsb[q][0:NC9, :], OB[q][0:NC9, :], ACT.Copy).then_inc(s["sel_done"], 1)
                modulation_loops(act, pair)
                act.wait_ge(s["modT_done"], layer + 1)
                for k in range(KT + 1):
                    if k < KT:
                        act.wait_ge(s["xT_full"], layer * KT + k + 1)
                        at_least(act, s["hT_done"], layer * KT + k - 1)
                        act.activation(hf[k % 2][:, 0:SMP], T[k % 2][:, 0:SMP], ACT.Identity,
                                       scale=modT[:, KT + k, 0:1], bias=modT[:, k, 0:1]).then_inc(s["h_prompt"], 1)
                    if k:
                        act.wait_ge(s["h_done"], layer * KT + k)
                        act.activation(hT[0][:, k - 1, :], hf[(k - 1) % 2], ACT.Copy).then_inc(s["hT_hi_done"], 1)
                for q in range(2):
                    act.wait_ge(gate_out[q], 32 * (layer + 1))

            def tail(yi, yb, blocks):
                for q in range(blocks):
                    act.wait_ge(s["yb_full"], yi + (q + 1))
                    act.activation(yT[0][:, bass.ds(yb + q, 1), :],
                                   T[q % 2][:, 0:NTOK].rearrange("p (o n) -> p o n", o=1), ACT.Copy,
                                   scale=0.5).then_inc(s["yb_hi"], 1)

            def gmlp(h, r, ai, yi, yb, oi):
                splits(r)
                splits(r + 1)
                for t in range(NT):
                    acc_ready(act, t, ai, r + 1)
                    act.activation(va[:, t, :], acc[:, t, :], ACT.Gelu_apprx_tanh).then_inc(acc_out[t], 1)
                splits(r + 2)
                splits(r + 3)
                for t in range(NT):
                    acc_ready(act, t, ai + 1, r + 3)
                    act.activation(ug[:, t, :], acc[:, t, :], ACT.Gelu_apprx_tanh).then_inc(acc_out[t], 1)
                splits(r + 4)
                splits(r + 5)
                for t in range(NT):
                    acc_ready(act, t, ai + 2, r + 5)
                    act.activation(wz[:, t, :], acc[:, t, :], ACT.Tanh, scale=0.5).then_inc(s["z_tanh"], 1)
                tail(yi, yb, 4)
                act.wait_ge(s["va_out"], h * 16 + 16)

            def out(kind, pn, kb, r, ai, yi, oi, last):
                if last:
                    split(r, 0)
                else:
                    splits(r)

            def ret(h, r, ai, yi, yb, oi):
                splits(r)
                splits(r + 1)
                split(r + 2, 0)
                split(r + 2, 1)
                for t in range(NT):
                    act.wait_ge(s["qkT_full"], h * NT + (t + 1))
                    if t == 0:
                        at_least(act, s["x_added"], oi * NT + LEAD)
                    act.activation(qkT[:, :, P * t:P * t + P], T[t % 2][:, :].rearrange("p (q n) -> p q n", q=4),
                                   ACT.Copy).then_inc(s["qkT_done"], 1)
                split(r + 2, 2)
                split(r + 2, 3)
                splits(r + 3)
                for t in range(NT):
                    acc_ready(act, t, ai + 1, r + 3)
                    if t == 0:
                        act.wait_ge(s["y_done"], h * NT + Z_RT + LEAD)
                    act.activation(vb[:, t, :], acc[:, t, 0:DVB], ACT.Copy).then_inc(s["v_done"], 1)
                    act.activation(wb[:, t, :], acc[:, t, DVB:W], ACT.Tanh, scale=0.5).then_inc(s["z_tanh"], 1)
                act.wait_ge(s["pst_full"], h + 1)
                act.activation(pst, T[1][:, :].rearrange("p (k v) -> p k v", k=KH), ACT.Copy)\
                   .then_inc(s["pst_done"], 1)
                tail(yi, yb, 2)
                act.wait_ge(s["pst_out"], h * 16 + 16)

            def gla_setup():
                act.wait_ge(s["lrw_in"], 16)
                act.activation(wlr[0], wlr_raw, ACT.Copy).then_inc(s["lrw_hi"], 1)
                act.wait_ge(s["lr_full"], 1)
                act.activation(lr_tok, OB[0][:, 0:NT * RANK].rearrange("p (t n) -> p t n", t=NT),
                               ACT.Copy).then_inc(s["lr_tok_done"], 1)
                act.wait_ge(s["lrT_full"], 1)
                act.wait_ge(s["ones_done"], 1)
                act.activation(lrT[0:RANK, :], OB[1][0:RANK, 0:NTOK], ACT.Copy).then_inc(s["lrT_done"], 1)
                act.wait_ge(s["pst_out"], 16 * B_HEADS)

            def gla(h, r, ai, yi, yb, oi):
                splits(r)
                for kt in range(KH):
                    act.wait_ge(s["gk_full"], h * KH + (kt + 1) + LEAD)
                    act.activation(ee[:, kt, :], OB[kt][:, 0:NTOK], ACT.Abs)
                act.drain()
                act.activation(ee, ee, ACT.Exp, scale=-1.0)
                act.drain()
                act.activation(ee, ee, ACT.Ln, bias=1.0).then_inc(s["gk_ln"], 1)
                splits(r + 1)
                for t in range(NT):
                    acc_ready(act, t, ai, r + 1)
                    act.activation(vc[:, t, :], acc[:, t, :], ACT.Copy).then_inc(acc_out[t], 1)
                act.wait_ge(s["dif_done"], h * 2 + 1)
                act.wait_ge(s["x_added"], oi * NT + LEAD)
                for sign, dst in ((GATE, qd), (-GATE, kd)):
                    act.activation(dst[:, :, 0:SMP], ee[:, :, 0:SMP], ACT.Exp, scale=sign)
                    last = act.activation(dst[:, :, SMP:NTOK], bb[:, :, SMP:NTOK], ACT.Exp, scale=sign)
                last.then_inc(s["exp_done"], 1)
                split(r + 2, 0)
                for n in range(2):
                    level_exp(n)
                act.drain()
                for kt in range(KH):
                    act.activation(ee[:, kt, 0:SMP], bb[:, kt, 0:SMP], ACT.Exp, scale=-GATE, bias=bend[:, kt:kt + 1])
                act.activation(ee[:, :, SMP:NTOK], ee[:, :, SMP:NTOK], ACT.Exp, scale=-GATE)
                act.activation(eb, bb[:, :, SMP:NTOK].rearrange("p k (b l) -> p k b l", l=LS)[:, :, :, LS - 1],
                               ACT.Exp, scale=GATE).then_inc(s["exp_done"], 1)
                for t in range(NT):
                    act.wait_ge(s["qkT_full"], h * NT + (B_HEADS * NT + t + 1))
                    v = T[t % 2][:, :].rearrange("p (q n) -> p q n", q=4)
                    act.activation(qkTc[:, 0:KH, P * t:P * t + P], v[:, 0:KH, :], ACT.Copy, scale=DK ** -0.5)
                    act.activation(qkTc[:, KH:2 * KH, P * t:P * t + P], v[:, KH:2 * KH, :], ACT.Copy)\
                       .then_inc(s["qkT_done"], 1)
                    if t < 2:
                        split(r + 2, 1 + t)
                split(r + 2, 3)
                split(r + 3, 0)
                act.wait_ge(s["dif_done"], h * 2 + 2)
                level_exp(2)
                split(r + 3, 1)
                act.wait_ge(s["kt_full"], h * 2 + 1)
                act.activation(ktok[:, 0:2, :], T[0][:, :].rearrange("p (t d) -> p t d", t=2), ACT.Copy)\
                   .then_inc(s["kt_done"], 1)
                act.wait_ge(s["kt_full"], h * 2 + 2)
                act.activation(ktok[:, 2, :], T[1][:, 0:DK], ACT.Copy, scale=parity[:, 0:1])
                act.activation(koc, T[1][:, 0:DK], ACT.Copy, scale=parity[:, 1:2]).then_inc(s["kt_done"], 1)
                split(r + 3, 2)
                split(r + 3, 3)
                for t in range(NT):
                    acc_ready(act, t, ai + 1, r + 3)
                    act.activation(vc[:, t, :], acc[:, t, :], ACT.Copy).then_inc(acc_out[t], 1)
                split(r + 4, 0)
                for kt in range(KH):
                    act.wait_ge(s["pst_full"], h * KH + (B_HEADS + kt + 1))
                    act.activation(pstc[:, kt, :], T[kt][:, :], ACT.Copy).then_inc(s["pst_done"], 1)
                for j in range(1, NSLOT):
                    split(r + 4, j)
                splits(r + 5)
                for t in range(NT):
                    acc_ready(act, t, ai + 2, r + 5)
                    act.wait_ge(s["y_done"], h * NT + (Z_GL + max(t - 1, 0)) + LEAD)
                    act.activation(wc[t % 2], acc[:, t, :], ACT.Tanh, scale=0.5).then_inc(s["z_tanh"], 1)
                tail(yi, yb, 4)

            def level_exp(n):
                w = 64 << n
                v = lev[n % 2].rearrange("p k (n w) -> p k n w", w=w)
                for kt in range(KH):
                    act.activation(v[:, kt, :, 0:w // 2], v[:, kt, :, 0:w // 2], ACT.Exp, scale=-GATE)
                    last = act.activation(v[:, kt, :, w // 2:w], v[:, kt, :, w // 2:w], ACT.Exp, scale=GATE)
                last.then_inc(s["exp_done"], 1)

            walk(act, dict(start=start, modulation=modulation, gmlp=gmlp, ret_setup=nothing, ret=ret,
                           gla_setup=gla_setup, gla=gla, out=out, finish=nothing))

        @block.vector
        def _(dve):
            def split(r, j):
                jj, rr = (j + AHEAD) % NSLOT, r + (j + AHEAD) // NSLOT
                dve.wait_ge(s["hi_ready"], 4 * rr + (jj + 1))
                dve.tensor_tensor(wlo[jj][:, :, :], raw[jj][:, :, :], whi[jj][:, :, :].bitcast(F32),
                                  ALU.subtract).then_inc(s["lo_ready"], 1)

            def splits(r):
                for j in range(NSLOT):
                    split(r, j)

            def start():
                lead(dve, [s["sel_done"], s["va_done"], s["mix_done"], s["sT_done"], s["o_done"], *acc_out])
                for j in range(AHEAD):
                    dve.wait_ge(s["hi_ready"], j + 1)
                    dve.tensor_tensor(wlo[j][:, :, :], raw[j][:, :, :], whi[j][:, :, :].bitcast(F32),
                                      ALU.subtract).then_inc(s["lo_ready"], 1)
                dve.wait_ge(s["th_done"], 1)
                dve.scalar_tensor_tensor(out=crow2[0:NC9, :], in0=crow2[0:NC9, :], scalar=1.0, in1=crow[0:NC9, :],
                                         op0=ALU.add, op1=ALU.mult).then_inc(s["cs_done"], 1)
                dve.wait_ge(s["ws_in"], 16 * (1 + NB))
                dve.memset(ws_nat[0:64, :, 64:P], 0.0).then_inc(s["ws_masked"], 1)
                dve.wait_ge(s["bs_in"], 16 * (1 + NB))

            def norm(pieces, src, n, scale=None):
                aggregate(pieces, src)
                dve.tensor_tensor(sq, mean_var[:, :, 0], mean_var[:, :, 0], ALU.mult)
                dve.drain()
                dve.tensor_tensor(ms, sq, mean_var[:, :, 1], ALU.add)
                dve.drain()
                if scale is not None:
                    dve.tensor_tensor(ms, ms, scale, ALU.mult)
                    dve.drain()
                dve.tensor_scalar(ms, ms, EPS, None, ALU.add).then_inc(s["ms_done"], 1)
                dve.wait_ge(s["rstd_done"], n + 1)

            def aggregate(pieces, src):
                for t in range(NT):
                    for q in range(pieces):
                        dve.bn_stats(stats[:, t, q, :], src(t, q))
                dve.drain()
                for t in range(NT):
                    dve.bn_aggr(small[:, 2 * t:2 * t + 2], stats[:, t, 0:pieces, :])
                dve.drain()

            def modulation(layer):
                if layer == 0:
                    dve.wait_ge(s["x_in"], 32)
                else:
                    dve.wait_ge(s["x_added"], NT * O_GL + LEAD)
                norm(4, lambda t, q: x[:, t, W * q:W * q + W], 0 if layer == 0 else 1 + A_HEADS + B_HEADS)
                dve.wait_ge(s["ident_done"], 1)
                for t in range(NT):
                    last = dve.tensor_scalar(diag[:, t, :], ident[:, :], rstd[:, t:t + 1], None, ALU.mult)
                last.then_inc(s["diag_done"], 1)
                dve.wait_ge(s["cTf_done"], 1)
                dve.tensor_copy(cT, zero.rearrange("p (a b) -> p a b", a=1).to_broadcast([P, KT, P]))
                dve.drain()
                dve.tensor_copy(cT[:, :, 0:NC9], cTf[:, :, :])
                dve.drain()
                dve.tensor_tensor(cT[:, :, LOROW:LOROW + NC9], cTf[:, :, :], cT[:, :, 0:NC9].bitcast(F32),
                                  ALU.subtract).then_inc(s["cT_done"], 1)

                def pair(mh, i, gate):
                    for q in range(2):
                        for half in range(2):
                            splits(mh * 4 + (R_MOD[layer] + 2 * q + half))
                    if not gate:
                        for q in range(2):
                            dve.wait_ge(s["sel_full"], mh * 2 + (12 * layer + q + 1) + LEAD)
                            dve.tensor_copy(modT[:, bass.ds(mh * 8 + 4 * q, 4), :],
                                            OB[q][:, 0:40].rearrange("p (c n) -> p c n", c=4))\
                               .then_inc(s["sel_done"], 1)
                modulation_loops(dve, pair)
                dve.drain()
                dve.scalar_tensor_tensor(out=modT[:, KT:2 * KT, 0:NC9], in0=modT[:, KT:2 * KT, 0:NC9], scalar=1.0,
                                         in1=modT[:, KT:2 * KT, NC9:10].to_broadcast([P, KT, NC9]),
                                         op0=ALU.add, op1=ALU.mult).then_inc(s["modT_done"], 1)
                dve.drain()

                def per_stream(k):
                    return modT[:, k, 1:NC9].rearrange("p (b o) -> p b o", o=1).to_broadcast([P, NB, LS])
                for k in range(KT + 1):
                    if k < KT:
                        dve.wait_ge(s["h_prompt"], layer * KT + k + 1)
                        hs = hf[k % 2][:, SMP:NTOK].rearrange("p (b l) -> p b l", b=NB)
                        dve.tensor_tensor(hs, T[k % 2][:, SMP:NTOK].rearrange("p (b l) -> p b l", b=NB),
                                          per_stream(KT + k), ALU.mult)
                        dve.drain()
                        dve.tensor_tensor(hs, hs, per_stream(k), ALU.add).then_inc(s["h_done"], 1)
                    if k:
                        dve.wait_ge(s["hT_hi_done"], layer * KT + k)
                        dve.tensor_tensor(hT[1][:, k - 1, :], hf[(k - 1) % 2], hT[0][:, k - 1, :].bitcast(F32),
                                          ALU.subtract).then_inc(s["hT_done"], 1)

            def tail(yi, yb, blocks):
                for q in range(blocks):
                    dve.wait_ge(s["yb_hi"], yi + (q + 1))
                    dve.scalar_tensor_tensor(out=yT[1][:, bass.ds(yb + q, 1), :],
                                             in0=T[q % 2][:, 0:NTOK].rearrange("p (o n) -> p o n", o=1), scalar=0.5,
                                             in1=yT[0][:, bass.ds(yb + q, 1), :].bitcast(F32),
                                             op0=ALU.mult, op1=ALU.subtract).then_inc(s["yb_lo"], 1)

            def silu(z0, th, z):
                for t in range(NT):
                    dve.wait_ge(s["z_tanh"], z0 + (t + 1))
                    dve.scalar_tensor_tensor(out=th(t), in0=th(t), scalar=1.0, in1=z(t),
                                             op0=ALU.add, op1=ALU.mult).then_inc(acc_out[t], 1)

            def gmlp(h, r, ai, yi, yb, oi):
                dve.wait_ge(s["wsT_done"], 2)
                dve.drain()
                at_least(dve, s["mix_full"], h * NT + LEAD)
                dve.tensor_copy(wsT, wsT_all[:, bass.ds(h, 1), :, :].rearrange("p o i t -> p (o i) t"))
                dve.tensor_copy(bs_cur, bsT[:, :, bass.ds(h, 1)].rearrange("p i o -> p (i o)"))\
                   .then_inc(s["wcur_done"], 1)
                splits(r)
                splits(r + 1)
                for t in range(NT):
                    dve.wait_ge(acc_out[t], ai + 1 + LEAD)
                aggregate(1, lambda t, q: va[:, t, :])
                dve.tensor_scalar(ms, mean_var[:, :, 1], EPS, None, ALU.add).then_inc(s["ms_done"], 1)
                dve.wait_ge(s["rstd_done"], h + 2)
                for t in range(NT):
                    dve.tensor_scalar(va[:, t, :], va[:, t, :], mean_var[:, t, 0:1], rstd[:, t:t + 1],
                                      ALU.subtract, ALU.mult)
                dve.drain()
                dve.wait_ge(s["ln_in"], h * 16 + 16)
                for t in range(NT):
                    dve.tensor_tensor(va[:, t, :], va[:, t, :], ln_g, ALU.mult).then_inc(s["va_done"], 1)
                splits(r + 2)
                splits(r + 3)
                splits(r + 4)
                for t in range(NT):
                    dve.wait_ge(s["mix_full"], h * NT + (t + 1) + LEAD)
                    dve.wait_ge(acc_out[t], ai + 2 + LEAD)
                    dve.scalar_tensor_tensor(out=ug[:, t, :], in0=(OB[0], OB[1], SC)[t][:, :],
                                             scalar=bs_cur[:, t // 2:t // 2 + 1], in1=ug[:, t, :],
                                             op0=ALU.add, op1=ALU.mult).then_inc(s["mix_done"], 1)
                splits(r + 5)
                silu(h * NT, lambda t: wz[:, t, :], lambda t: acc[:, t, :])
                tail(yi, yb, 4)

            def out(kind, pn, kb, r, ai, yi, oi, last):
                if last:
                    split(r, 0)
                else:
                    splits(r)
                dve.wait_ge(s["g_in"], oi * 32 + 32)
                for t in range(NT):
                    acc_ready(dve, t, ai, r)
                    at_least(dve, s["x_added"], oi * NT + (t - 2) + LEAD)
                    dve.tensor_tensor(out_tmp[kind][:, t, :], acc[:, t, :], out_g[kind][:, t // 2, :], ALU.mult)\
                       .then_inc(acc_out[t], 1)

            def ret_setup():
                dve.wait_ge(s["rt_const"], 16 * 5)
                dve.tensor_copy(mask_u, mask01)

            def ret(h, r, ai, yi, yb, oi):
                dve.drain()
                dve.tensor_copy(hc, hc_all[:, bass.ds(h, 1), :].rearrange("p o c -> p (o c)"))
                splits(r)
                splits(r + 1)
                for t in range(NT):
                    dve.drain()
                    acc_ready(dve, t, ai, r + 1)
                    if t == 0:
                        dve.wait_ge(s["yb_full"], yi)
                    v = acc[:, t, :].rearrange("p (q e n) -> p q e n", q=2, e=2)
                    sv = swp.rearrange("p (q e n) -> p q e n", q=2, e=2)
                    sn_t = sn[:, t:t + 1, :].to_broadcast([P, 2, P])
                    dve.tensor_tensor(qkr[:, t, :].rearrange("p (q n) -> p q n", q=4),
                                      acc[:, t, :].rearrange("p (q n) -> p q n", q=4),
                                      cs[:, t:t + 1, :].to_broadcast([P, 4, P]), ALU.mult)
                    dve.tensor_tensor(sv[:, :, 0, :], v[:, :, 1, :], sn_t, ALU.mult)
                    dve.tensor_tensor(sv[:, :, 1, :], v[:, :, 0, :], sn_t, ALU.mult).then_inc(acc_out[t], 1)
                    dve.drain()
                    o = qkr[:, t, :].rearrange("p (q e n) -> p q e n", q=2, e=2)
                    dve.tensor_tensor(o[:, :, 0, :], o[:, :, 0, :], sv[:, :, 0, :], ALU.subtract)
                    dve.tensor_tensor(o[:, :, 1, :], o[:, :, 1, :], sv[:, :, 1, :], ALU.add).then_inc(s["rot_done"], 1)
                splits(r + 2)
                dve.wait_ge(s["qkT_full"], h * NT + NT)
                k2 = qkr[:, 2, DK:2 * DK]
                dve.tensor_scalar(kob, k2, hc[:, HC_KO:HC_KO + 1], None, ALU.mult)
                for t in range(2):
                    kt_ = qkr[:, t, DK:2 * DK]
                    dve.tensor_scalar(kt_, kt_, hc[:, HC_K + t:HC_K + t + 1], None, ALU.mult)
                dve.drain()
                dve.tensor_scalar(k2, k2, hc[:, HC_KE:HC_KE + 1], None, ALU.mult).then_inc(s["kd_done"], 1)
                splits(r + 3)
                dve.wait_ge(s["sc_full"], h + 1)
                for n, (c0, c1) in enumerate(((0, 256), (256, 384), (384, 512))):
                    last = dve.scalar_tensor_tensor(out=sTb[:, c0:c1], in0=SC[:, c0:c1],
                                                    scalar=hc[:, HC_PW + n:HC_PW + n + 1], in1=mask01[:, c0:c1],
                                                    op0=ALU.mult, op1=ALU.mult)
                last.then_inc(s["sT_done"], 1)
                silu(h * NT + Z_RT, lambda t: wb[:, t, :], lambda t: acc[:, t, DVB:W])
                for c in range(CH_RT):
                    for i in range(2):
                        dve.wait_ge(s["up_full"], h * (2 * CH_RT) + (2 * c + i + 1))
                        half = state[c][:, W * i:W * i + W]
                        dve.scalar_tensor_tensor(out=half, in0=half, scalar=hc[:, HC_S:HC_S + 1], in1=T[i][:, :],
                                                 op0=ALU.mult, op1=ALU.add).then_inc(s["up_done"], 1)
                dve.wait_ge(s["o_full"], h * 2 + 2)

                def o_tile(t):
                    return OB[0][:, DVB * t:DVB * t + DVB] if t < 2 else OB[1][:, 0:DVB]
                norm(1, lambda t, q: o_tile(t), h + (1 + A_HEADS), hc[:, HC_Q2:HC_Q2 + NT])
                dve.tensor_tensor(fac, rstd, hc[:, HC_Q:HC_Q + NT], ALU.mult)
                dve.drain()
                for t in range(NT):
                    dve.scalar_tensor_tensor(out=onb[:, t, :], in0=o_tile(t), scalar=fac[:, t:t + 1], in1=ret_g,
                                             op0=ALU.mult, op1=ALU.mult).then_inc(s["o_done"], 1)
                tail(yi, yb, 2)

            def gla_setup():
                dve.wait_ge(s["lrw_hi"], 1)
                dve.tensor_tensor(wlr[1], wlr_raw, wlr[0].bitcast(F32), ALU.subtract).then_inc(s["lrw_done"], 1)
                dve.drain()
                dve.memset(sTc, 0.0)
                dve.wait_ge(s["gl_const"], 48)
                dve.wait_ge(s["pst_out"], 16 * B_HEADS)

            def level_diff(n):
                w = 64 << n
                v = lev[n % 2].rearrange("p k (n w) -> p k n w", w=w)
                b = bb[:, :, 0:SMP].rearrange("p k (n w) -> p k n w", w=w)
                for kt in range(KH):
                    last = dve.tensor_tensor(v[:, kt], b[:, kt],
                                             b[:, kt, :, w // 2 - 1:w // 2].to_broadcast([P, SMP // w, w]),
                                             ALU.subtract)
                return last

            def level_mult(n):
                w = 64 << n
                v = lev[n % 2].rearrange("p k (n w) -> p k n w", w=w)
                q = qkTc[:, 0:KH, 0:SMP].rearrange("p k (n w) -> p k n w", w=w)
                k = qkTc[:, KH:2 * KH, 0:SMP].rearrange("p k (n w) -> p k n w", w=w)
                for kt in range(KH):
                    dve.tensor_tensor(v[:, kt, :, 0:w // 2], v[:, kt, :, 0:w // 2], k[:, kt, :, 0:w // 2], ALU.mult)
                    last = dve.tensor_tensor(v[:, kt, :, w // 2:w], v[:, kt, :, w // 2:w], q[:, kt, :, w // 2:w],
                                             ALU.mult)
                last.then_inc(s["dec_done"], 1)

            def gla(h, r, ai, yi, yb, oi):
                splits(r)
                dve.wait_ge(s["gk_ln"], h + 1)
                for kt in range(KH):
                    dve.scalar_tensor_tensor(out=ee[:, kt, :], in0=OB[kt][:, 0:NTOK], scalar=0.0, in1=ee[:, kt, :],
                                             op0=ALU.min, op1=ALU.subtract).then_inc(s["gk_done"], 1)
                dve.drain()
                for kt in range(KH):
                    dve.tensor_tensor_scan(bb[:, kt, :], smask, ee[:, kt, :], 0.0, ALU.mult, ALU.add)
                dve.drain()
                dve.tensor_scalar(bend, bb[:, :, SMP - 1], GATE, None, ALU.mult)
                dve.wait_ge(s["pst_out"], h * 16 + 16 * B_HEADS)
                level_diff(0)
                level_diff(1)
                b32 = bb[:, :, 0:SMP].rearrange("p k (n w) -> p k n w", w=32)
                e32 = ee[:, :, 0:SMP].rearrange("p k (n w) -> p k n w", w=32)
                b16 = bb[:, :, SMP:NTOK].rearrange("p k (n w) -> p k n w", w=LS)
                e16 = ee[:, :, SMP:NTOK].rearrange("p k (n w) -> p k n w", w=LS)
                for kt in range(KH):
                    dve.tensor_tensor(e16[:, kt], b16[:, kt], b16[:, kt, :, LS - 1:LS].to_broadcast([P, NB, LS]),
                                      ALU.subtract)
                    last = dve.tensor_tensor(e32[:, kt], b32[:, kt], b32[:, kt, :, 15:16].to_broadcast([P, 8, 32]),
                                             ALU.subtract)
                last.then_inc(s["dif_done"], 1)
                splits(r + 1)
                split(r + 2, 0)
                split(r + 2, 1)
                dve.wait_ge(s["qkT_done"], h * NT + (B_HEADS + 1) * NT)
                dve.wait_ge(s["exp_done"], h * 5 + 4)
                dve.tensor_tensor(qd, qd, qkTc[:, 0:KH, :], ALU.mult)
                dve.tensor_tensor(kd, kd, qkTc[:, KH:2 * KH, :], ALU.mult).then_inc(s["dec_done"], 1)
                level_mult(0)
                level_mult(1)
                dve.tensor_tensor(ee, ee, qkTc[:, KH:2 * KH, :], ALU.mult).then_inc(s["dec_done"], 1)
                split(r + 2, 2)
                split(r + 2, 3)
                dve.wait_ge(s["lev_used"], h + 1)
                level_diff(2).then_inc(s["dif_done"], 1)
                split(r + 3, 0)
                dve.wait_ge(s["exp_done"], h * 5 + 5)
                level_mult(2)
                split(r + 3, 1)
                split(r + 3, 2)
                dve.wait_ge(s["sc_full"], h + (B_HEADS + 1))
                apart(dve)
                dve.copy_predicated(sTc, mask_u, SC[:, :]).then_inc(s["sT_done"], 1)
                split(r + 3, 3)
                for c in range(CH_GL):
                    split(r + 4 + c // NSLOT, c % NSLOT)
                    for i in range(2):
                        b = 2 * (c % 4) + i
                        dve.wait_ge(s["up_full"], h * (2 * CH_GL) + (2 * N_RT + 2 * c + i + 1))
                        half = state[c % NST][:, W * i:W * i + W]
                        dve.scalar_tensor_tensor(out=half, in0=half, scalar=eb[:, c // 4, b:b + 1], in1=T[i][:, :],
                                                 op0=ALU.mult, op1=ALU.add).then_inc(s["up_done"], 1)
                dve.wait_ge(s["o_full"], h * 2 + (2 * B_HEADS + 2))
                o_banks = (OB[0], OB[1], SC)
                norm(1, lambda t, q: o_banks[t][:, :], h + (2 + A_HEADS + B_HEADS))
                for t in range(NT):
                    dve.scalar_tensor_tensor(out=onc[:, t, :], in0=o_banks[t][:, :], scalar=rstd[:, t:t + 1],
                                             in1=gla_g, op0=ALU.mult, op1=ALU.mult).then_inc(s["o_done"], 1)
                silu(h * NT + Z_GL, lambda t: wc[t % 2], lambda t: acc[:, t, :])
                tail(yi, yb, 4)

            def finish():
                dve.wait_ge(s["x_added"], NT * 32 + LEAD)
                norm(4, lambda t, q: x[:, t, W * q:W * q + W], 2 + A_HEADS + B_HEADS + C_HEADS)
                dve.wait_ge(s["fg_in"], 16)
                for t in range(NT):
                    dve.scalar_tensor_tensor(out=x[:, t, :], in0=x[:, t, :], scalar=rstd[:, t:t + 1],
                                             in1=work[:, 0:D], op0=ALU.mult, op1=ALU.mult).then_inc(s["final_done"], 1)

            walk(dve, dict(start=start, modulation=modulation, gmlp=gmlp, ret_setup=ret_setup, ret=ret,
                           gla_setup=gla_setup, gla=gla, out=out, finish=finish))

        @block.tensor
        def _(pe):
            def mm(out, lhsT, rhs, start=True, stop=True):
                return pe.matmul(out, lhsT, rhs, start=start, stop=stop, skip_group_check=True)

            def granule(r, j, lhs, k0, first, last, ai):
                pe.wait_ge(s["lo_ready"], 4 * r + (j + 1))
                for t in range(NT):
                    if first:
                        at_least(pe, acc_out[t], ai + LEAD)
                    for k in range(GK):
                        a_hi, a_lo = (part[:, k0 + k, P * t:P * t + P] for part in lhs)
                        mm(acc[:, t, :], a_hi, whi[j][:, k, :], first and k == 0, False)
                        mm(acc[:, t, :], a_hi, wlo[j][:, k, :], False, False)
                        ins = mm(acc[:, t, :], a_lo, whi[j][:, k, :], False, last and k == GK - 1)
                    if last and t < 2:
                        ins.then_inc(s["acc_full"], 1)
                ins.then_inc(s["w_used"], 1)

            def project(r, ai, steps={}):
                for g in range(2 * NSLOT):
                    granule(r + g // NSLOT, g % NSLOT, hT, GK * g, g == 0, g == 2 * NSLOT - 1, ai)
                    if g in steps:
                        steps[g]()

            def start():
                lead(pe, [s["w_used"], s["sel_full"], s["mix_full"], s["gk_full"]])
                pe.wait_ge(s["ident_done"], 1)
                pe.wait_ge(s["cs_done"], 1)
                for k in range(KT):
                    ins = pe.transpose(SC[:, NC9 * k:NC9 * k + NC9], crow2[0:NC9, P * k:P * k + P], ident[0:NC9, 0:NC9])
                ins.then_inc(s["cTf_full"], 1)
                pe.wait_ge(s["ws_masked"], 1)
                for i, src in enumerate((ws_nat, ws_diag)):
                    for h in range(A_HEADS):
                        ins = pe.transpose(OB[i][:, P * h:P * h + P], src[:, h, :], ident[:, :])
                    ins.then_inc(s["wsT_full"], 1)
                pe.wait_ge(s["const_in"], 16)
                pe.wait_ge(s["wsT_done"], 2)

            def modulation(layer):
                pe.wait_ge(s["cT_done"], layer + 1)

                def pair(mh, i, gate):
                    for q in range(2):
                        for g in range(2 * NSLOT):
                            r, j = mh * 4 + (R_MOD[layer] + 2 * q + g // NSLOT), g % NSLOT
                            pe.wait_ge(s["lo_ready"], 4 * r + (j + 1))
                            if g == 0:
                                at_least(pe, s["modsb_done"], mh * 2 + (12 * layer + q - 1) + LEAD)
                            for k in range(GK):
                                kk = GK * g + k
                                mm(T[q][:, :], cT[:, kk, :], whi[j][:, k, :], kk == 0, False)
                                ins = mm(T[q][:, :], cT[:, kk, :], wlo[j][:, k, :], False, kk == KT - 1)
                            if g < 2 * NSLOT - 1:
                                ins.then_inc(s["w_used"], 1)
                            else:
                                ins.then_inc(s["mod_full"], 1)
                        release(mh * 2 + (12 * layer + q + 1))
                    for q in range(2):
                        pe.wait_ge(s["modsb_done"], mh * 2 + (12 * layer + q + 1) + LEAD)
                        pe.wait_ge(rows_in[q], mh * 32 + (6 * layer + 1) * 32)
                        at_least(pe, s["sel_done"], mh * 2 + (12 * layer + q - 1) + LEAD)
                        if gate:
                            ins = mm(OB[q][0:NC9, :], sel[0:NROW, 0:NC9], modsb[q][0:NROW, :])
                        else:
                            for c in range(4):
                                ins = mm(OB[q][:, 10 * c:10 * c + 10], modsb[q][0:NROW, P * c:P * c + P], sel[0:NROW, :])
                        ins.then_inc(s["sel_full"], 1)

                def release(n):
                    mm(SC[0:1, 0:1], ident[0:1, 0:1], ident[0:1, 0:1]).then_inc(s["w_used"], 1)
                modulation_loops(pe, pair)
                pe.wait_ge(s["diag_done"], layer + 1)
                pe.wait_ge(s["modsb_done"], 12 * layer + 12 + LEAD)
                for k in range(KT):
                    at_least(pe, s["h_done"], layer * KT + k - 1)
                    for t in range(NT):
                        ins = mm(T[k % 2][:, P * t:P * t + P], x[:, t, P * k:P * k + P], diag[:, t, :])
                    ins.then_inc(s["xT_full"], 1)
                pe.wait_ge(s["hT_done"], KT * (layer + 1))

            def tail(yi, y, y_need, blocks):
                pe.wait_ge(s["y_done"], y_need + LEAD)
                for q in range(blocks):
                    if q >= 2:
                        pe.wait_ge(s["yb_lo"], yi + (q - 1))
                    for t in range(NT):
                        ins = pe.transpose(T[q % 2][:, P * t:P * t + P], y[:, t, P * q:P * q + P], ident[:, :])
                    ins.then_inc(s["yb_full"], 1)
                pe.wait_ge(s["yb_lo"], yi + blocks)

            def gmlp(h, r, ai, yi, yb, oi):
                project(r, ai)
                project(r + 2, ai + 1)

                def mix():
                    pe.wait_ge(s["va_done"], h * NT + NT + LEAD)
                    pe.wait_ge(s["wcur_done"], h + 1)
                    at_least(pe, s["mix_done"], h * NT + LEAD)
                    for t in range(NT):
                        mm((OB[0], OB[1], SC)[t][:, :], wsT[:, t // 2, :], va[:, t, :]).then_inc(s["mix_full"], 1)
                project(r + 4, ai + 2, {3: mix})
                tail(yi, ug, h * NT + NT, 4)

            def out(kind, pn, kb, r, ai, yi, oi, last):
                for g in range(NSLOT):
                    granule(r, g, yT, GK * g, g == 0, g == NSLOT - 1, ai)

            def ret_setup():
                pe.wait_ge(s["mix_done"], NT * A_HEADS + LEAD)

            def ret(h, r, ai, yi, yb, oi):
                project(r, ai)

                def turn(t):
                    pe.wait_ge(s["rot_done"], h * NT + (t + 1))
                    if t == 2:
                        pe.wait_ge(s["qkT_done"], h * NT + 1)
                    for q in range(4):
                        ins = pe.transpose(T[t % 2][:, P * q:P * q + P], qkr[:, t, P * q:P * q + P], ident[:, :])
                    ins.then_inc(s["qkT_full"], 1)

                def first_turns():
                    turn(0)
                    turn(1)

                def scores():
                    pe.wait_ge(s["qkT_done"], h * NT + NT)
                    at_least(pe, s["sT_done"], h + LEAD)
                    for k0, q0, n, c0 in ((0, 0, 256, 0), (128, 128, 128, 256), (256, 256, 128, 384)):
                        for kt in range(KH):
                            ins = mm(SC[:, c0:c0 + n], qkT[:, KH + kt, k0:k0 + P], qkT[:, kt, q0:q0 + n],
                                     kt == 0, kt == KH - 1)
                    ins.then_inc(s["sc_full"], 1)
                project(r + 2, ai + 1, {1: first_turns, 2: lambda: turn(2), 5: scores})
                pe.wait_ge(s["sT_done"], h + 1 + LEAD)
                pe.wait_ge(s["v_done"], h * NT + NT)
                at_least(pe, s["o_done"], h * NT + LEAD)
                mm(OB[0][:, 0:DVB], sTb[:, 0:P], vb[:, 0, :])
                mm(OB[0][:, DVB:W], sTb[:, P:2 * P], vb[:, 0, :], True, False)
                mm(OB[0][:, DVB:W], sTb[:, 2 * P:3 * P], vb[:, 1, :], False, True).then_inc(s["o_full"], 1)
                pe.wait_ge(s["kd_done"], h + 1)
                for kt in range(KH):
                    for t in range(2):
                        ins = mm(T[1][:, DVB * kt:DVB * kt + DVB], qkr[:, t, DK + P * kt:DK + P * kt + P],
                                 vb[:, t, :], t == 0, t == 1)
                ins.then_inc(s["pst_full"], 1)
                mm(OB[1][:, 0:DVB], sTb[:, 3 * P:4 * P], vb[:, 2, :], True, False)
                pe.wait_ge(s["qm_done"], h + 1)
                for c in range(CH_RT):
                    kt = c // 2
                    pe.wait_ge(st_in[c], h * 16 + 16)
                    for i in range(4):
                        b = 4 * (c % 2) + i
                        g0 = 32 * (b // 2)
                        ins = mm(OB[1][g0:g0 + 32, 0:DVB], qmask[:, kt, b, :], state[c][:, DVB * i:DVB * i + DVB],
                                 False, c >= 2)
                    if c == CH_RT - 1:
                        ins.then_inc(s["o_full"], 1)
                    for i in range(2):
                        g0 = 32 * (2 * (c % 2) + i)
                        if c:
                            pe.wait_ge(s["up_done"], h * (2 * CH_RT) + (2 * c - 1 + i))
                        elif i:
                            pe.wait_ge(s["pst_done"], h + 1)
                        for e, k_tok in enumerate((qkr[:, 2, DK:2 * DK], kob)):
                            ins = mm(T[i][:, DVB * e:DVB * e + DVB], k_tok[g0:g0 + 32, P * kt:P * kt + P],
                                     vb[g0:g0 + 32, 2, :])
                        ins.then_inc(s["up_full"], 1)
                pe.wait_ge(s["up_done"], h * (2 * CH_RT) + 2 * CH_RT)
                tail(yi, onb, h * NT + (Z_RT + NT), 2)

            def gla_setup():
                pe.wait_ge(s["lrw_done"], 1)
                pe.wait_ge(s["o_done"], NT * B_HEADS + LEAD)
                for t in range(NT):
                    for k in range(KT):
                        for n, (hp, wp) in enumerate(((0, 0), (0, 1), (1, 0))):
                            ins = mm(OB[0][:, RANK * t:RANK * t + RANK], hT[hp][:, k, P * t:P * t + P], wlr[wp][:, k, :],
                                     k == 0 and n == 0, k == KT - 1 and n == 2)
                ins.then_inc(s["lr_full"], 1)
                pe.wait_ge(s["lr_tok_done"], 1)
                for t in range(NT):
                    ins = pe.transpose(OB[1][0:RANK, P * t:P * t + P], lr_tok[:, t, :], ident[:, :])
                ins.then_inc(s["lrT_full"], 1)
                pe.wait_ge(s["lrT_done"], 1)

            def gla(h, r, ai, yi, yb, oi):
                def gates():
                    pe.wait_ge(s["gkw_in"], h * 32 + 32)
                    pe.wait_ge(s["o_done"], h * NT + B_HEADS * NT + LEAD)
                    for kt in range(KH):
                        mm(OB[kt][:, 0:NTOK], gkw[0:RANK + 1, P * kt:P * kt + P], lrT[0:RANK + 1, :])\
                            .then_inc(s["gk_full"], 1)
                project(r, ai, {0: gates})

                def turn(t):
                    pe.wait_ge(acc_out[t], ai + 1 + LEAD)
                    if t == 2:
                        pe.wait_ge(s["qkT_done"], h * NT + (B_HEADS * NT + 1))
                    for q in range(4):
                        ins = pe.transpose(T[t % 2][:, P * q:P * q + P], vc[:, t, P * q:P * q + P], ident[:, :])
                    ins.then_inc(s["qkT_full"], 1)

                def first_turns():
                    turn(0)
                    turn(1)

                def block_scores(key, query, k0, k1, q0, q1, c0):
                    row = k0 % P
                    for kt in range(KH):
                        ins = mm(SC[row:row + k1 - k0, c0:c0 + q1 - q0], key[:, kt, k0:k1], query[:, kt, q0:q1],
                                 kt == 0, kt == KH - 1)
                    return ins

                def diagonal():
                    pe.wait_ge(s["dec_done"], h * 5 + 1)
                    for t in range(2):
                        for i in range(4):
                            k0 = P * t + 32 * i
                            block_scores(kd, qd, k0, k0 + 32, k0, k0 + 32, 256 * t + 32 * i)
                    block_scores(kd, qd, SMP, NTOK, SMP, NTOK, 384)

                def level(n):
                    w = 64 << n
                    v = lev[n % 2]
                    pe.wait_ge(s["dec_done"], h * 5 + (2, 3, 5)[n])
                    for m in range(SMP // w):
                        a0, mid = m * w, m * w + w // 2
                        t = a0 // P
                        c0 = mid if n == 2 else 256 * t + mid - P * t
                        ins = block_scores(v, v, a0, mid, mid, a0 + w, c0)
                    return ins

                def key_tails():
                    pe.wait_ge(s["dec_done"], h * 5 + 4)
                    pe.wait_ge(s["qkT_done"], h * NT + (B_HEADS + 1) * NT)
                    for t in range(NT):
                        for kt in range(KH):
                            c0 = DK * (t % 2) + P * kt
                            ins = pe.transpose(T[t // 2][:, c0:c0 + P], ee[:, kt, P * t:P * t + P], ident[:, :])
                        if t:
                            ins.then_inc(s["kt_full"], 1)

                project(r + 2, ai + 1, {
                    0: first_turns, 1: lambda: turn(2), 2: diagonal,
                    3: lambda: level(0).then_inc(s["lev_used"], 1), 4: lambda: level(1), 5: key_tails,
                    6: lambda: level(2).then_inc(s["sc_full"], 1)})

                def prompt():
                    for t in range(NT):
                        pe.wait_ge(acc_out[t], ai + 2 + LEAD)
                    pe.wait_ge(s["sT_done"], h + (B_HEADS + 1) + LEAD)
                    pe.wait_ge(s["gk_done"], h * KH + KH)
                    mm(OB[0][:, :], sTc[:, 0:P], vc[:, 0, :])
                    mm(OB[1][:, :], sTc[:, P:2 * P], vc[:, 0, :], True, False)
                    mm(OB[1][:, :], sTc[:, 2 * P:3 * P], vc[:, 1, :], False, True).then_inc(s["o_full"], 1)
                    pe.wait_ge(s["kt_done"], h * 2 + 2)
                    for kt in range(KH):
                        for t in range(2):
                            ins = mm(T[kt][:, :], ktok[:, t, P * kt:P * kt + P], vc[:, t, :], t == 0, t == 1)
                        ins.then_inc(s["pst_full"], 1)
                    mm(SC[:, :], sTc[:, 3 * P:4 * P], vc[:, 2, :], True, False)
                    pe.wait_ge(s["qm_done"], h + (B_HEADS + 1))

                def piece(c):
                    kt, g0 = c // 4, 32 * (c % 4)
                    pe.wait_ge(st_in[c % NST], h * 32 + 16 * (B_HEADS + c // NST + 1))
                    for i in range(2):
                        ins = mm(SC[g0:g0 + 32, :], qmask[:, kt, 2 * (c % 4) + i, :], state[c % NST][:, W * i:W * i + W],
                                 False, c >= 4)
                    if c == CH_GL - 1:
                        ins.then_inc(s["o_full"], 1)
                    for i, k_tok in enumerate((ktok[:, 2, :], koc)):
                        if c:
                            pe.wait_ge(s["up_done"], h * (2 * CH_GL) + (2 * N_RT + 2 * c - 1 + i))
                        else:
                            pe.wait_ge(s["pst_done"], h * KH + (B_HEADS + 1 + i))
                        mm(T[i][:, :], k_tok[g0:g0 + 32, P * kt:P * kt + P], vc[g0:g0 + 32, 2, :])\
                            .then_inc(s["up_full"], 1)

                def first_piece():
                    prompt()
                    piece(0)
                steps = {0: first_piece}
                for c in range(1, CH_GL):
                    steps[c] = lambda c=c: piece(c)
                project(r + 4, ai + 2, steps)
                pe.wait_ge(s["up_done"], h * (2 * CH_GL) + (2 * N_RT + 2 * CH_GL))
                tail(yi, onc, h * NT + (Z_GL + NT), 4)

            walk(pe, dict(start=start, modulation=modulation, gmlp=gmlp, ret_setup=ret_setup, ret=ret,
                          gla_setup=gla_setup, gla=gla, out=out, finish=nothing))


def shape_constants():
    f32 = np.float32
    pos = np.concatenate([np.arange(256), np.tile(PAST + np.arange(LS), NB)]).astype(f32)
    freqs = f32(10000.0) ** (-np.arange(P, dtype=f32) / f32(P))
    ang = (pos[:, None] * freqs[None, :]).astype(f32)
    turned = [f(ang.astype(np.float64)).astype(f32).reshape(NT, P, P).transpose(1, 0, 2) for f in (np.cos, np.sin)]

    p = np.arange(P)
    i = p % LS
    causal = (p[None, :] >= p[:, None])
    same = (p[None, :] // LS) == (p[:, None] // LS)
    mask = np.concatenate([causal, np.ones((P, P), bool), causal, causal & same], axis=1)

    lg = np.log1p(-np.exp2(-5.0 - np.arange(B_HEADS)))
    hc = np.zeros((P, B_HEADS, 16), np.float64)
    for h in range(B_HEADS):
        g = lambda n: np.exp(lg[h] * n)
        sc = DK ** -0.5
        hc[:, h, HC_PW] = g(-(p + 1.0)) * sc
        hc[:, h, HC_PW + 1] = g(-(p + 129.0)) * sc
        hc[:, h, HC_PW + 2] = g(-(i + 1.0)) * sc
        for t, n in enumerate((p + 1.0, p + 129.0, i + 1.0)):
            hc[:, h, HC_Q + t] = g(n)
            hc[:, h, HC_Q2 + t] = g(2 * n)
        hc[:, h, HC_K] = g(255.0 - p) * sc
        hc[:, h, HC_K + 1] = g(127.0 - p) * sc
        even = (p // LS) % 2 == 0
        hc[:, h, HC_KE] = g(15.0 - i) * sc * even
        hc[:, h, HC_KO] = g(15.0 - i) * sc * ~even
        hc[:, h, HC_S] = g(16.0)
    sel = np.zeros((P, 10), f32)
    for c in range(NC9):
        sel[[c, LOROW + c, BROW], c] = 1.0
    sel[GROW, NC9] = 1.0
    scan = np.ones((P, NTOK), f32)
    scan[:, 0] = 0.0
    scan[:, 256::LS] = 0.0
    parity = np.stack([(p // LS) % 2 == 0, (p // LS) % 2 == 1], axis=1).astype(f32)
    return {"cos": turned[0], "sin": turned[1], "mask01": mask.astype(f32),
            "hc": hc.astype(f32), "sel": sel, "scan_mask": scan, "parity": parity}


_INS = ["x_prompt", "x_sample", "state_ret", "state_gla", "c_prompt", "c_sample", "norm_g", "w_mod", "b_mod", "w_in_e",
        "gmlp_ln_g", "gmlp_ws", "gmlp_bs", "ret_norm_g", "w_out_e", "w_in_o", "w_gk2", "b_gk", "gla_norm_g", "w_out_o",
        "final_g"]
_OUTS = [(1, 256, D), (NB, LS, D), (1, 1, B_HEADS, DK, DVB), (1, NB, B_HEADS, DK, DVB), (1, 1, C_HEADS, DK, DVC),
         (1, NB, C_HEADS, DK, DVC), (1, NB, LS, D)]


def kernel(**inputs):
    import concourse.bacc as bacc
    from concourse.bass_utils import run_bass_kernel_spmd

    nc = bacc.Bacc("TRN2", target_bir_lowering=False, num_devices=1)
    arrays = {}

    def dram_in(name, array):
        array = np.ascontiguousarray(array)
        arrays[name] = array
        return nc.dram_tensor(name, array.shape, mybir.dt.from_np(array.dtype), kind="ExternalInput").ap()

    args = {n: dram_in(f"in_{n}", inputs[n]) for n in _INS}
    consts = {n: dram_in(f"const_{n}", v) for n, v in shape_constants().items()}
    outs = [nc.dram_tensor(f"out_{i}", s, F32, kind="ExternalOutput").ap() for i, s in enumerate(_OUTS)]
    build(nc, args, consts, outs)
    r = run_bass_kernel_spmd(nc, [arrays], core_ids=[0])
    return tuple(r.results[0][f"out_{i}"] for i in range(len(_OUTS)))
```

```python
from contextlib import ExitStack

import numpy as np

import concourse.bass as bass
from concourse import mybir
from concourse.alu_op_type import AluOpType as ALU

F32 = mybir.dt.float32
F32R = mybir.dt.float32r
U8 = mybir.dt.uint8
ACT = mybir.ActivationFunctionType

P = 128
D = 2048
KT = D // P
NB = 8
LS = 16
NT = 3
NTOK = NT * P
SMP = 2 * P
W = 512
PAST = 128
A_HEADS, B_HEADS, C_HEADS = 4, 8, 8
DK = 256
DVB, DVC = 256, 512
KH = DK // P
RANK = 16
GATE = 1 / 16.0
EPS = 1e-6
NC9 = 1 + NB
LOROW = 16
CROW = 32
BROW, GROW = 32, 33
NROW = 34

NSLOT = 4
GK = 2
LEAD = 16
AHEAD = 3
R_MOD = (0, 96)
R_GM, R_RT, R_GL = 24, 72, 120
A_GM, A_RT, A_GL = 0, 20, 44
Y_GM, Y_RT, Y_GL = 0, 16, 32
O_GM, O_RT, O_GL = 0, 8, 16
Z_RT, Z_GL = NT * A_HEADS, NT * (A_HEADS + B_HEADS)
YB = 8
NST = 4
CH_RT, CH_GL = 4, 8
N_RT = CH_RT * B_HEADS

HC_PW, HC_Q, HC_Q2, HC_K, HC_KE, HC_KO, HC_S = 0, 3, 6, 9, 11, 12, 13


def build(nc, a, consts, outs):
    y_p, y_s, ret_p, ret_s, gla_p, gla_s, gmlp_v = outs
    gate_dram = nc.dram_tensor("gate_rows", [2, NC9, D], F32, kind="Internal").ap()

    w_e = a["w_in_e"][0].rearrange("(k p) n -> p k n", p=P)
    w_o = a["w_in_o"][0].rearrange("(k p) n -> p k n", p=P)
    wo = [a["w_out_e"][0].rearrange("(k p) n -> p k n", p=P), a["w_out_o"][0].rearrange("(k p) n -> p k n", p=P)]
    w_m = [a["w_mod"][l].rearrange("(k p) n -> p k n", p=P) for l in range(2)]
    b_m = a["b_mod"]
    v_rows = gmlp_v[0].rearrange("b l d -> (b l) d")
    st_r, st_g = a["state_ret"][0], a["state_gla"][0]

    with ExitStack() as ctx:
        def sb(name, shape, dt=F32):
            return ctx.enter_context(nc.sbuf_tensor(name, shape, dt))

        def bank(name, shape):
            return ctx.enter_context(nc.psum_tensor(name, shape, F32))

        def sem(name):
            return ctx.enter_context(nc.semaphore(name))

        acc = bank("acc", [P, NT, W])
        T = [bank("turn0", [P, W]), bank("turn1", [P, W])]
        SC = bank("scores", [P, W])
        OB = [bank("mixed0", [P, W]), bank("mixed1", [P, W])]

        raw = [sb(f"raw{j}", [P, GK, W]) for j in range(NSLOT)]
        whi = [sb(f"whi{j}", [P, GK, W], F32R) for j in range(NSLOT)]
        wlo = [sb(f"wlo{j}", [P, GK, W], F32R) for j in range(NSLOT)]
        hT = [sb("hT_hi", [P, KT, NTOK], F32R), sb("hT_lo", [P, KT, NTOK], F32R)]
        yT = [sb("yT_hi", [P, YB, NTOK], F32R), sb("yT_lo", [P, YB, NTOK], F32R)]
        x = sb("x", [P, NT, D])
        ident = sb("ident", [P, P])
        sel = sb("sel", [P, 10])
        modT = sb("modT", [P, 2 * KT, 10])
        cT = sb("cT", [P, KT, CROW], F32R)
        small = sb("small", [P, 32])
        stats = sb("stats", [P, NT, 4, 6])
        cst = sb("cst", [P, 4])
        state = [sb(f"state{s}", [P, 1024]) for s in range(NST)]
        qmask = sb("qmask", [P, KH, NB, 32])
        work = sb("work", [P, 10646])
        neg_half, zero = cst[:, 0:3], cst[:, 3:4]
        mean_var = small[:, 0:6].rearrange("p (t c) -> p t c", c=2)
        sq, ms, rstd, fac = small[:, 8:11], small[:, 12:15], small[:, 16:19], small[:, 20:23]

        def carve(at, *shape):
            v = work[:, at:at + int(np.prod(shape))]
            if len(shape) == 2:
                v = v.rearrange("p (a b) -> p a b", a=shape[0])
            if len(shape) == 3:
                v = v.rearrange("p (a b c) -> p a b c", a=shape[0], b=shape[1])
            return v

        diag = carve(0, NT, P)
        modsb = [carve(7680 + W * i, W) for i in range(2)]
        gsb = [carve(1536 + W * i, W) for i in range(2)]
        hf = [carve(2560 + NTOK * i, NTOK) for i in range(2)]
        crow = carve(3584, D)
        cTf, cth = carve(10100, KT, NC9), carve(10244, KT, NC9)
        ws_nat, ws_diag = carve(512, A_HEADS, P), carve(1024, A_HEADS, P)
        wsT_all = carve(8704, A_HEADS, 2, P)
        bsT = carve(9728, 2, A_HEADS)
        va, ug, wz = carve(0, NT, W), carve(1536, NT, W), carve(3072, NT, W)
        ln_g = carve(4608, W)
        wsT = carve(9744, 2, P)
        bs_cur = carve(10000, 2)
        cs, sn = carve(0, NT, P), carve(384, NT, P)
        mask01 = carve(768, W)
        hc_all, hc = carve(1280, B_HEADS, 16), carve(1408, 16)
        ret_g = carve(1424, DVB)
        qkr = carve(1680, NT, W)
        qkT = carve(3216, 2 * KH, NTOK)
        swp = carve(4752, W)
        sTb = carve(5264, W)
        vb, wb = carve(5776, NT, DVB), carve(6544, NT, DVB)
        onb = carve(7312, NT, DVB)
        kob = carve(8080, DK)
        pst = carve(8336, KH, DVB)
        C0 = 8980
        mask_u = carve(C0, P).bitcast(U8)
        smask = carve(C0 + 128, NTOK)
        gla_g = carve(C0 + 512, W)
        parity = carve(C0 + 1024, 2)
        lrT = carve(C0 + 1026, NTOK)
        wlr_raw, koc = carve(C0 + 1410, KT, RANK), carve(C0 + 1410, DK)
        gkw = carve(0, DK)
        eb, bend = carve(256, KH, NB), carve(272, KH)
        qkTc = carve(276, 2 * KH, NTOK)
        onc = carve(276, NT, W)
        bb = carve(1812, KH, NTOK)
        ktok = carve(1812, NT, DK)
        qd, kd = carve(2580, KH, NTOK), carve(3348, KH, NTOK)
        lev = [carve(4116, KH, 2 * P), carve(4628, KH, 2 * P)]
        pstc = carve(4116, KH, DVC)
        ee = carve(5140, KH, NTOK)
        vc = carve(5908, NT, W)
        wc = [carve(7444, W), carve(7956, W), carve(3348, W)]
        sTc = carve(8468, W)
        flat = [t[:, :, :].rearrange("p a b -> p (a b)")[:, 0:KT * RANK].rearrange("p (k c) -> p k c", k=KT) for t in yT]
        wlr = flat
        out_tmp = {"gm": carve(5120, NT, W), "rt": carve(3216, NT, W), "gl": carve(2580, NT, W)}
        out_g = {"gm": carve(6656, 2, W), "rt": carve(5776, 2, W), "gl": carve(4116, 2, W)}

        names = """passed hi_ready lo_ready w_used acc_full const_in ws_in bs_in x_in c_in ident_done
            cT_full th_done cT_done zero_done ws_zero ws_masked wsT_full wsT_done
            modsb_done sel_full sel_done ms_done rstd_done diag_done modT_done
            xT_full h_prompt h_done hT_hi_done hT_done
            ln_in wcur_done va_done va_out mix_full mix_done z_tanh y_done yb_full yb_hi yb_lo g_in x_added
            rt_const rot_done qkT_full qkT_done sc_full sT_done kd_done qm_done v_done o_full o_done
            pst_full pst_done pst_out up_full up_done
            gl_const lrw_in lrw_hi lrw_done lrT_full ones_done lrT_done gkw_in gk_full gk_ln
            gk_done dif_done exp_done dec_done lev_used kt_full kt_done fg_in final_done y_out""".split()
        s = {n: sem(n) for n in names}
        raw_in = [sem(f"raw_in{j}") for j in range(NSLOT)]
        acc_out = [sem(f"acc_out{t}") for t in range(NT)]
        rows_in = [sem(f"rows_in{q}") for q in range(2)]
        gate_out = [sem(f"gate_out{q}") for q in range(2)]
        st_in = [sem(f"st_in{i}") for i in range(NST)]
        st_out = [sem(f"st_out{i}") for i in range(NST)]

        def at_least(eng, sm, n):
            if not isinstance(n, int) or n > 0:
                eng.wait_ge(sm, n)

        def acc_ready(eng, t, ai, r, j=3):
            if t < 2:
                eng.wait_ge(s["acc_full"], 2 * ai + t + 1)
            else:
                eng.wait_ge(s["w_used"], 4 * r + (j + 1 + LEAD))

        def turn_bank(q, wide):
            return (T[0], T[1], OB[0], OB[1])[q] if wide else T[q % 2]

        def walk(eng, e):
            e["start"]()
            e["modulation"](0)

            def gmlp_head(ph, hh, before):
                e["gmlp"](ph * 2 + hh, hh, ph * 24 + (hh * 10 + R_GM), ph * 10 + hh * 3 + A_GM, before)

            def ret_head(ph, hh, before):
                e["ret"](ph * 4 + hh, hh * 4 + (ph * 20 + R_RT), hh * 2 + (ph * 12 + A_RT), ph * 4 + O_RT, before)

            def gla_head(ph, hh, before):
                e["gla"](ph * 2 + hh, ph * 16 + (hh * 6 + R_GL), ph * 10 + (hh * 3 + A_GL), ph * 4 + O_GL, before)

            def out_panel(kind, ph, pn, before, last=False):
                kb, r, ai, yi, oi = {
                    "gm": (ph * 8, ph * 24 + (R_GM + 20), ph * 10 + (A_GM + 6), ph * 8 + (Y_GM + YB), ph * 4 + O_GM),
                    "rt": (ph * 8 + 16, ph * 20 + (R_RT + 16), ph * 12 + (A_RT + 8), ph * 8 + (Y_RT + YB), ph * 4 + O_RT),
                    "gl": (ph * 8, ph * 16 + (R_GL + 12), ph * 10 + (A_GL + 6), ph * 8 + (Y_GL + YB), ph * 4 + O_GL),
                }[kind]
                e["out"](kind, pn, kb, pn + r, pn + ai, yi, pn + oi, last, before)

            def out_panels(kind, ph, before):
                out_panel(kind, ph, 0, before)
                with eng.Fori(1, 4) as pn:
                    out_panel(kind, ph, pn, None)

            with eng.Fori(0, 2) as ph:
                gmlp_head(ph, 0, None)
                gmlp_head(ph, 1, ("gm", ph * 2, ph * 8 + Y_GM, 0))
                out_panels("gm", ph, ("gm", ph * 2 + 1, ph * 8 + (Y_GM + 4), 4))
            e["ret_setup"]()
            with eng.Fori(0, 2) as ph:
                ret_head(ph, 0, None)
                with eng.Fori(0, 3) as hh:
                    ret_head(ph, hh + 1, ("rt", ph * 4 + hh, ph * 8 + hh * 2 + Y_RT, hh * 2))
                out_panels("rt", ph, ("rt", ph * 4 + 3, ph * 8 + (Y_RT + 6), 6))
            e["modulation"](1)
            e["gla_setup"]()

            def gla_heads(ph):
                gla_head(ph, 0, None)
                gla_head(ph, 1, ("gl", ph * 2, ph * 8 + Y_GL, 0))

            with eng.Fori(0, 3) as ph:
                gla_heads(ph)
                out_panels("gl", ph, ("gl", ph * 2 + 1, ph * 8 + (Y_GL + 4), 4))
            gla_heads(3)
            out_panel("gl", 3, 0, ("gl", 7, 3 * 8 + (Y_GL + 4), 4))
            with eng.Fori(1, 3) as pn:
                out_panel("gl", 3, pn, None)
            out_panel("gl", 3, 3, None, True)
            e["finish"]()

        def modulation_loops(eng, pair, layer):
            if layer == 0:
                pair(0, False, None)
                with eng.Fori(1, 4) as mh:
                    pair(mh, False, mh - 1)
            pair(4, True, None if layer else 3)
            pair(5, True, 4)

        def x_block(n):
            if n >= 28:
                return n - 16
            return (n - 5) // 2 if n % 2 and n >= 5 else None

        def nothing(*_):
            pass

        def apart(eng):
            eng.sem_inc(s["passed"], 1)

        def lead(eng, sems):
            for sm in sems:
                eng.sem_inc(sm, LEAD)

        ctx.enter_context(nc.allow_non_contiguous_dma(reason="the offsets of the mixing, a few hundred numbers"))
        block = ctx.enter_context(nc.Block())

        @block.sync
        def _(sp):
            def load(r, j, src):
                at_least(sp, s["lo_ready"], 4 * r + (j - 3))
                if not isinstance(r, int):
                    apart(sp)
                for k in range(GK):
                    dst, part = raw[j][:, k, :], src[:, k]
                    if len(part.shape) == 3:
                        dst = dst.rearrange("p (s n) -> p s n", s=2)
                    sp.dma_start(dst, part).then_inc(raw_in[j], 16)

            def panel(r, src):
                for q in range(2):
                    for j in range(NSLOT):
                        load(r + q, j, src(8 * q + GK * j))

            def start():
                sp.dma_start(crow[0:1, :], a["c_prompt"]).then_inc(s["c_in"], 16)
                sp.dma_start(crow[1:NC9, :], a["c_sample"]).then_inc(s["c_in"], 16)

            def modulation(layer):
                def pair(mh):
                    for q in range(2):
                        for half in range(2):
                            for j in range(NSLOT):
                                r = mh * 4 + (R_MOD[layer] + 2 * q + half)
                                k = 8 * half + GK * j
                                load(r, j, w_m[layer][:, k:k + GK, bass.ds(mh * (2 * W) + q * W, W)])
                if layer == 0:
                    first_pair(pair)
                else:
                    with sp.Fori(4, 6) as mh:
                        pair(mh)

            def first_pair(pair):
                for q in range(2):
                    for half in range(2):
                        for j in range(NSLOT):
                            load(2 * q + half, j, w_m[0][:, 8 * half + GK * j:8 * half + GK * j + GK, q * W:q * W + W])
                with sp.Fori(1, 6) as mh:
                    pair(mh)

            def gmlp(h, hh, r, ai, before):
                for q, part in enumerate((1, 0)):
                    for g in range(2 * NSLOT):
                        k, rr, j = GK * g, r + (4 * q + g // 2), 2 * (g % 2)
                        load(rr, j, w_e[:, k:k + GK, bass.ds(h * W + part * D, W)])
                        load(rr, j + 1, w_m[1][:, k:k + GK, bass.ds(h * (2 * W) + q * W, W)])
                panel(r + 8, lambda k: w_e[:, k:k + GK, bass.ds(h * W + 2 * D, W)])

            def two_projections(w, c0, gap, h):
                def src(k):
                    v = w[:, k:k + GK, c0:c0 + 2 * gap].rearrange("p k (s n) -> p k s n", s=2)
                    return v[:, :, :, bass.ds(h * DK, DK)]
                return src

            def ret(h, r, ai, oi, before):
                panel(r, two_projections(w_e, 3 * D, D, h))
                panel(r + 2, two_projections(w_e, 5 * D, D, h))

            def gla(h, r, ai, oi, before):
                panel(r, two_projections(w_o, 0, D, h))
                panel(r + 2, lambda k: w_o[:, k:k + GK, bass.ds(h * W + 2 * D, W)])
                panel(r + 4, lambda k: w_o[:, k:k + GK, bass.ds(h * W + 4 * D, W)])

            def out(kind, pn, kb, r, ai, yi, oi, last, before):
                layer = int(kind == "gl")
                for j in range(NSLOT):
                    load(r, j, wo[layer][:, bass.ds(kb + GK * j, GK), bass.ds(pn * W, W)])

            def finish():
                for t in range(NT):
                    sp.wait_ge(s["final_done"], t + 1)
                    dst = y_s.rearrange("b l d -> (b l) d") if t == 2 else y_p[0, P * t:P * t + P, :]
                    sp.dma_start(dst, x[:, t, :]).then_inc(s["y_out"], 16)
                sp.wait_ge(s["y_out"], 16 * NT)
                sp.wait_ge(s["va_out"], 16 * A_HEADS)
                sp.wait_ge(s["pst_out"], 16 * (B_HEADS + C_HEADS))
                for i in range(NST):
                    sp.wait_ge(st_out[i], 16 * (B_HEADS + 2 * C_HEADS))

            walk(sp, dict(start=start, modulation=modulation, gmlp=gmlp, ret_setup=nothing, ret=ret,
                          gla_setup=nothing, gla=gla, out=out, finish=finish))

        @block.gpsimd
        def _(pool):
            def start():
                lead(pool, [s["x_added"], s["y_done"]])
                pool.memset(cst[:, 0:3], -0.5)
                pool.memset(cst[:, 3:4], 0.0).then_inc(s["zero_done"], 1)
                pool.memset(ident[:, :], 0.0)
                pool.drain()
                pool.affine_select(out=ident[:, :], in_=ident[:, :], compare_op=ALU.not_equal, fill=1.0, base=0,
                                   pattern=[[-1, P]], channel_multiplier=1).then_inc(s["ident_done"], 1)
                pool.dma_start(sel[:, :], consts["sel"]).then_inc(s["const_in"], 16)
                pool.memset(qmask[:, :, :, :], 0.0)
                pool.memset(ws_diag, 0.0).then_inc(s["ws_zero"], 1)
                pool.dma_start(x[:, 0:2, :], a["x_prompt"][0].rearrange("(t p) d -> p t d", p=P)).then_inc(s["x_in"], 16)
                pool.dma_start(x[:, 2, :], a["x_sample"].rearrange("b l d -> (b l) d")).then_inc(s["x_in"], 16)
                pool.dma_start(ws_nat, a["gmlp_ws"][0].rearrange("h t s -> t h s")).then_inc(s["ws_in"], 16)
                pool.wait_ge(s["ws_zero"], 1)
                for b in range(NB):
                    pool.dma_start(ws_diag[LS * b:LS * b + LS, :, LS * b:LS * b + LS],
                                   a["gmlp_ws"][0, :, 0:LS, 0:LS].rearrange("h t s -> t h s")).then_inc(s["ws_in"], 16)
                    pool.dma_start(bsT[LS * b:LS * b + LS, 1, :],
                                   a["gmlp_bs"][0, :, 0:LS].rearrange("h t -> t h")).then_inc(s["bs_in"], 16)
                pool.dma_start(bsT[:, 0, :], a["gmlp_bs"][0].rearrange("h t -> t h")).then_inc(s["bs_in"], 16)

            def rsqrt(n):
                pool.wait_ge(s["ms_done"], n)
                pool.tensor_tensor(rstd, ms, neg_half, ALU.pow).then_inc(s["rstd_done"], 1)

            def modulation(layer):
                if layer == 0:
                    with pool.Fori(0, 2) as kind:
                        with pool.Fori(0, 2) as i:
                            mod_rows(0, kind * 2 + i, i)
                rsqrt(1 if layer == 0 else 2 + A_HEADS + B_HEADS)
                done = 0
                for i in range(2):
                    mh = 4 + i
                    mod_rows(layer, mh, i)
                    for q in range(2):
                        for k in range(done, (4, 8, 12, 16)[2 * i + q]):
                            pool.wait_ge(s["hT_hi_done"], layer * KT + k + 1)
                            pool.tensor_tensor(hT[1][:, k, :], hf[k % 2], hT[0][:, k, :].bitcast(F32),
                                               ALU.subtract).then_inc(s["hT_done"], 1)
                        done = k + 1
                        pool.wait_ge(s["sel_done"], mh * 2 + (12 * layer + q + 1) + LEAD)
                        pool.dma_start(gate_dram[layer, :, bass.ds(i * (2 * W) + q * W, W)], gsb[q][0:NC9, :])\
                            .then_inc(gate_out[q], 16)

            def mod_rows(layer, mh, i):
                for q in range(2):
                    at_least(pool, s["sel_full"], mh * 2 + (12 * layer + q - 1) + LEAD)
                    apart(pool)
                    pool.dma_start(modsb[q][BROW:BROW + 1, :], b_m[layer:layer + 1, bass.ds(mh * (2 * W) + q * W, W)])\
                        .then_inc(rows_in[q], 16)
                    pool.dma_start(modsb[q][GROW:GROW + 1, :],
                                   a["norm_g"][layer:layer + 1, bass.ds(i * (2 * W) + q * W, W)])\
                        .then_inc(rows_in[q], 16)

            def products(ai, y, gate_tile):
                for t in range(NT):
                    pool.wait_ge(acc_out[t], ai + LEAD)
                    pool.tensor_tensor(y[:, t, :], y[:, t, :], gate_tile(t), ALU.mult).then_inc(s["y_done"], 1)

            def gmlp(h, hh, r, ai, before):
                mod_rows(1, h, hh)
                at_least(pool, s["va_done"], h * NT + LEAD)
                apart(pool)
                pool.dma_start(ln_g, a["gmlp_ln_g"][0, bass.ds(h * W, W)].partition_broadcast(P)).then_inc(s["ln_in"], 16)
                rsqrt(h + 2)
                pool.wait_ge(s["va_done"], h * NT + NT + LEAD)
                apart(pool)
                pool.dma_start(v_rows[:, bass.ds(h * W, W)], va[:, 2, :]).then_inc(s["va_out"], 16)
                pool.wait_ge(s["mix_done"], h * NT + NT + LEAD)
                products(ai + 3, ug, lambda t: wz[:, t, :])

            def out(kind, pn, kb, r, ai, yi, oi, last, before):
                layer = int(kind == "gl")
                for q in range(2):
                    pool.wait_ge(gate_out[q], 32 * (layer + 1))
                pool.wait_ge(s["yb_full"], yi)
                if kind == "gl":
                    pool.wait_ge(s["pst_out"], kb * 4 + (16 * (B_HEADS + 2)))
                pool.wait_ge(acc_out[2], ai + LEAD)
                apart(pool)
                g = out_g[kind]
                pool.dma_start(g[:, 0, :], gate_dram[layer, 0, bass.ds(pn * W, W)].partition_broadcast(P))\
                    .then_inc(s["g_in"], 16)
                pool.dma_start(g[:, 1, :], gate_dram[layer, 1:NC9, bass.ds(pn * W, W)]
                               .rearrange("b (o n) -> b o n", o=1).to_broadcast([NB, LS, W])).then_inc(s["g_in"], 16)
                for t in range(NT):
                    pool.wait_ge(acc_out[t], ai + 1 + LEAD)
                    xs = x[:, t, bass.ds(pn * W, W)]
                    pool.tensor_tensor(xs, xs, out_tmp[kind][:, t, :], ALU.add).then_inc(s["x_added"], 1)

            def ret_setup():
                pool.wait_ge(s["x_added"], NT * O_RT + LEAD)
                for dst, src in ((cs, consts["cos"]), (sn, consts["sin"]), (mask01, consts["mask01"]),
                                 (hc_all, consts["hc"]), (ret_g, a["ret_norm_g"][0].partition_broadcast(P))):
                    pool.dma_start(dst, src).then_inc(s["rt_const"], 16)
                for dst, src in ((smask, consts["scan_mask"]), (parity, consts["parity"]),
                                 (gla_g, a["gla_norm_g"][0].partition_broadcast(P))):
                    pool.dma_start(dst, src).then_inc(s["gl_const"], 16)
                pool.dma_start(wlr_raw, w_o[:, :, 12288:12288 + RANK]).then_inc(s["lrw_in"], 16)

            def ret_piece(st, h, c):
                return st[4 * (c % 2):4 * (c % 2) + 4, bass.ds(h, 1),
                          P * (c // 2):P * (c // 2) + P, :].rearrange("b o p v -> p (b o) v")

            def gla_piece(st, h, c):
                return st[2 * (c % 4):2 * (c % 4) + 2, bass.ds(h, 1),
                          P * (c // 4):P * (c // 4) + P, :].rearrange("b o p v -> p (b o) v")

            def st_free(uses):
                for c in range(NST):
                    pool.wait_ge(st_out[c], uses * 16)
                apart(pool)

            def st_load(piece, src, h, c, n):
                pool.dma_start(state[c % NST][:, :].rearrange("p (b v) -> p b v", b=n), piece(src, h, c))\
                    .then_inc(st_in[c % NST], 16)

            def st_store(piece, dst, h, c, sc, n):
                pool.wait_ge(s["up_done"], sc * 2 + 2)
                apart(pool)
                pool.dma_start(piece(dst, h, c), state[c % NST][:, :].rearrange("p (b v) -> p b v", b=n))\
                    .then_inc(st_out[c % NST], 16)

            def spread_q(q_samples):
                for b2 in range(2):
                    qv = q_samples.rearrange("p k (b c l) -> p k b c l", c=2, l=LS)[:, :, :, b2, :]
                    dst = qmask[:, :, :, :].rearrange("p k (b c) l -> p k b c l", c=2)[:, :, :, b2, LS * b2:LS * b2 + LS]
                    for kt in range(KH):
                        last = pool.tensor_copy(dst[:, kt], qv[:, kt])
                last.then_inc(s["qm_done"], 1)

            def ret(h, r, ai, oi, before):
                for c in range(CH_RT):
                    st_load(ret_piece, st_r, h, c, 4)
                pool.wait_ge(s["qkT_done"], h * NT + NT)
                apart(pool)
                spread_q(qkT[:, 0:KH, SMP:NTOK])
                pool.wait_ge(s["pst_done"], h + 1)
                apart(pool)
                pool.dma_start(ret_p[0, 0, bass.ds(h, 1)].rearrange("o (k p) v -> p (o k) v", p=P), pst)\
                    .then_inc(s["pst_out"], 16)
                for c in range(CH_RT):
                    st_store(ret_piece, ret_s[0], h, c, h * CH_RT + c, 4)
                rsqrt(h + (2 + A_HEADS))
                pool.wait_ge(s["o_done"], h * NT + NT + LEAD)
                products(ai + 2, onb, lambda t: wb[:, t, :])
                st_free(h + 1)

            def gla_setup():
                pool.wait_ge(s["hT_done"], 2 * KT)
                pool.memset(lrT[0:32, :], 1.0).then_inc(s["ones_done"], 1)
                gate_weights(0)

            def gate_weights(h):
                pool.dma_start(gkw[0:RANK, :], a["w_gk2"][0, :, bass.ds(h * DK, DK)]).then_inc(s["gkw_in"], 16)
                pool.dma_start(gkw[RANK:RANK + 1, :], a["b_gk"][:, bass.ds(h * DK, DK)]).then_inc(s["gkw_in"], 16)

            def gla(h, r, ai, oi, before):
                for c in range(NST):
                    st_load(gla_piece, st_g, h, c, 2)
                pool.wait_ge(s["dec_done"], h * 5 + 1)
                apart(pool)
                spread_q(qd[:, :, SMP:NTOK])
                if not (isinstance(h, int) and h == C_HEADS - 1):
                    pool.wait_ge(s["gk_full"], h * KH + KH + LEAD)
                    apart(pool)
                    gate_weights(h + 1)
                pool.wait_ge(s["pst_done"], h * KH + (B_HEADS + KH))
                apart(pool)
                pool.dma_start(gla_p[0, 0, bass.ds(h, 1)].rearrange("o (k p) v -> p (o k) v", p=P), pstc)\
                    .then_inc(s["pst_out"], 16)
                for c in range(CH_GL):
                    st_store(gla_piece, gla_s[0], h, c, h * CH_GL + (N_RT + c), 2)
                    if 1 <= c <= NST:
                        pool.wait_ge(st_out[c - 1], h * 32 + 16 * (B_HEADS + 1))
                        apart(pool)
                        st_load(gla_piece, st_g, h, c - 1 + NST, 2)
                rsqrt(h + (3 + A_HEADS + B_HEADS))
                pool.wait_ge(s["o_done"], h * NT + (B_HEADS + 1) * NT + LEAD)
                products(ai + 3, onc, lambda t: wc[t])
                st_free(h * 2 + (B_HEADS + 2))

            def finish():
                pool.wait_ge(s["x_added"], NT * 32 + LEAD)
                apart(pool)
                pool.dma_start(work[:, 0:D], a["final_g"].partition_broadcast(P)).then_inc(s["fg_in"], 16)
                rsqrt(4 + A_HEADS + B_HEADS + C_HEADS - 1)

            walk(pool, dict(start=start, modulation=modulation, gmlp=gmlp, ret_setup=ret_setup, ret=ret,
                            gla_setup=gla_setup, gla=gla, out=out, finish=finish))

        @block.scalar
        def _(act):
            def split(r, j):
                jj, rr = (j + AHEAD) % NSLOT, r + (j + AHEAD) // NSLOT
                act.wait_ge(raw_in[jj], 32 * rr + 32)
                at_least(act, s["w_used"], 4 * r + j + LEAD)
                act.activation(whi[jj][:, :, :], raw[jj][:, :, :], ACT.Copy).then_inc(s["hi_ready"], 1)

            def splits(r):
                for j in range(NSLOT):
                    split(r, j)

            def start():
                lead(act, [s["modsb_done"]])
                act.wait_ge(s["cT_full"], 1)
                act.activation(cth, SC[:, 0:KT * NC9].rearrange("p (k c) -> p k c", k=KT), ACT.Tanh,
                               scale=0.5).then_inc(s["th_done"], 1)
                for j in range(AHEAD):
                    act.wait_ge(raw_in[j], 32)
                    act.activation(whi[j][:, :, :], raw[j][:, :, :], ACT.Copy).then_inc(s["hi_ready"], 1)

            def modulation(layer):
                if layer:
                    act.wait_ge(s["x_added"], NT * O_GL + LEAD)
                    act.wait_ge(s["lrw_in"], 16)
                    act.activation(wlr[0], wlr_raw, ACT.Copy).then_inc(s["lrw_hi"], 1)

                def panel_out(mh, q):
                    act.wait_ge(s["w_used"], mh * 16 + (4 * R_MOD[layer] + 8 * q + 8 + LEAD))
                    act.activation(modsb[q][0:CROW, :], T[q][0:CROW, :], ACT.Copy).then_inc(s["modsb_done"], 1)

                def gate_rows(mh, q):
                    act.wait_ge(s["sel_full"], mh * 2 + (12 * layer + q + 1) + LEAD)
                    at_least(act, gate_out[q], (mh - 4) * 16 + 32 * layer)
                    act.activation(gsb[q][0:NC9, :], OB[q][0:NC9, :], ACT.Copy).then_inc(s["sel_done"], 1)

                def pair(mh, gate, before):
                    for q in range(2):
                        last = (before, 1) if q == 0 else (mh, 0)
                        for g in range(2 * NSLOT):
                            split(mh * 4 + (R_MOD[layer] + 2 * q + g // NSLOT), g % NSLOT)
                            if g == 0 and last[0] is not None:
                                panel_out(*last)
                            if g == 3 and (gate if q else gate and mh == 5):
                                gate_rows(*last)
                            if not gate:
                                continue
                            n = 2 * NSLOT * (2 * (mh - 4) + q) + g
                            if layer == 0 and n in (10, 12):
                                act.wait_ge(s["wsT_full"], n // 2 - 4)
                                act.activation(wsT_all[:, :, n // 2 - 5, :],
                                               acc[:, 2, :].rearrange("p (h t) -> p h t", h=A_HEADS),
                                               ACT.Copy).then_inc(s["wsT_done"], 1)
                            if n == 31:
                                panel_out(5, 1)
                            if x_block(n) == 0:
                                act.wait_ge(s["modT_done"], layer + 1)
                            if x_block(n) is not None:
                                prompt_block(x_block(n))

                def prompt_block(k):
                    if k < KT:
                        act.wait_ge(s["xT_full"], layer * KT + k + 1)
                        at_least(act, s["hT_done"], layer * KT + k - 1)
                        act.activation(hf[k % 2][:, 0:SMP], acc[:, k % 2, 0:SMP], ACT.Identity,
                                       scale=modT[:, KT + k, 0:1], bias=modT[:, k, 0:1]).then_inc(s["h_prompt"], 1)
                    if k:
                        act.wait_ge(s["h_done"], layer * KT + k)
                        act.activation(hT[0][:, k - 1, :], hf[(k - 1) % 2], ACT.Copy).then_inc(s["hT_hi_done"], 1)
                modulation_loops(act, pair, layer)
                gate_rows(5, 1)
                prompt_block(KT)
                for q in range(2):
                    act.wait_ge(gate_out[q], 32 * (layer + 1))

            def turned(before, q0, wide=False):
                kind, h, yi, yb = before
                for q in (q0, q0 + 1):
                    src = turn_bank(q, wide)[:, 0:NTOK].rearrange("p (o n) -> p o n", o=1)
                    act.wait_ge(s["yb_full"], yi + (q + 1))
                    act.activation(yT[0][:, bass.ds(yb + q, 1), :],
                                   src, ACT.Copy, scale=0.5).then_inc(s["yb_hi"], 1)

            def ret_state(before):
                act.wait_ge(s["pst_full"], before[1] + 1)
                act.activation(pst, T[1][:, :].rearrange("p (k v) -> p k v", k=KH), ACT.Copy)\
                   .then_inc(s["pst_done"], 1)

            def gmlp(h, hh, r, ai, before):
                for q, (dst, use) in enumerate(((va, ai), (ug, ai + 1))):
                    rr = r + 4 * q
                    splits(rr)
                    splits(rr + 1)
                    if before and q == 0:
                        turned(before, 0)
                        turned(before, 2)
                        act.wait_ge(s["va_out"], before[1] * 16 + 16)
                    splits(rr + 2)
                    for j in range(3):
                        split(rr + 3, j)
                    for t in range(NT):
                        acc_ready(act, t, use, rr + 3, 2)
                        act.activation(dst[:, t, :], acc[:, t, :], ACT.Gelu_apprx_tanh).then_inc(acc_out[t], 1)
                    split(rr + 3, 3)
                    act.wait_ge(s["w_used"], 4 * rr + (16 + LEAD))
                    act.activation(modsb[q][0:CROW, :], OB[q][0:CROW, :], ACT.Copy).then_inc(s["modsb_done"], 1)
                splits(r + 8)
                splits(r + 9)
                for t in range(NT):
                    acc_ready(act, t, ai + 2, r + 9)
                    act.activation(wz[:, t, :], acc[:, t, :], ACT.Tanh, scale=0.5).then_inc(s["z_tanh"], 1)

            def out(kind, pn, kb, r, ai, yi, oi, last, before):
                split(r, 0)
                if last:
                    return
                if kind == "rt" and before:
                    ret_state(before)
                split(r, 1)
                if kind != "rt" and before:
                    turned(before, 0, True)
                    turned(before, 2, True)
                    if kind == "gm":
                        act.wait_ge(s["va_out"], before[1] * 16 + 16)
                split(r, 2)
                if kind == "rt" and before:
                    turned(before, 0, True)
                    act.wait_ge(s["pst_out"], before[1] * 16 + 16)
                split(r, 3)

            def ret(h, r, ai, oi, before):
                split(r, 0)
                if before:
                    ret_state(before)
                split(r, 1)
                split(r, 2)
                split(r, 3)
                split(r + 1, 0)
                split(r + 1, 1)
                split(r + 1, 2)
                if before:
                    turned(before, 0)
                    act.wait_ge(s["pst_out"], before[1] * 16 + 16)
                split(r + 1, 3)
                for t in range(NT):
                    acc_ready(act, t, ai, r + 1)
                    act.activation(qkr[:, t, :], acc[:, t, :], ACT.Copy).then_inc(acc_out[t], 1)
                split(r + 2, 0)
                split(r + 2, 1)
                for t in range(NT):
                    act.wait_ge(s["qkT_full"], h * NT + (t + 1))
                    if t == 0:
                        at_least(act, s["x_added"], oi * NT + LEAD)
                    act.activation(qkT[:, :, P * t:P * t + P], T[t % 2][:, :].rearrange("p (q n) -> p q n", q=4),
                                   ACT.Copy).then_inc(s["qkT_done"], 1)
                split(r + 2, 2)
                split(r + 2, 3)
                splits(r + 3)
                for t in range(NT):
                    acc_ready(act, t, ai + 1, r + 3)
                    if t == 0:
                        act.wait_ge(s["y_done"], h * NT + Z_RT + LEAD)
                    act.activation(vb[:, t, :], acc[:, t, 0:DVB], ACT.Copy).then_inc(s["v_done"], 1)
                    act.activation(wb[:, t, :], acc[:, t, DVB:W], ACT.Tanh, scale=0.5).then_inc(s["z_tanh"], 1)

            def gla_setup():
                act.wait_ge(s["lrT_full"], 1)
                act.wait_ge(s["ones_done"], 1)
                act.activation(lrT[0:RANK, :], SC[0:RANK, 0:NTOK], ACT.Copy).then_inc(s["lrT_done"], 1)
                act.wait_ge(s["pst_out"], 16 * B_HEADS)

            def gla(h, r, ai, oi, before):
                split(r, 0)
                split(r, 1)
                for kt in range(KH):
                    act.wait_ge(s["gk_full"], h * KH + (kt + 1) + LEAD)
                    act.activation(ee[:, kt, :], OB[kt][:, 0:NTOK], ACT.Abs)
                act.drain()
                act.activation(ee, ee, ACT.Exp, scale=-1.0)
                act.drain()
                act.activation(ee, ee, ACT.Ln, bias=1.0).then_inc(s["gk_ln"], 1)
                split(r, 2)
                if before:
                    turned(before, 0)
                split(r, 3)
                if before:
                    turned(before, 2)
                splits(r + 1)
                for t in range(NT):
                    acc_ready(act, t, ai, r + 1)
                    act.activation(vc[:, t, :], acc[:, t, :], ACT.Copy).then_inc(acc_out[t], 1)
                act.wait_ge(s["dif_done"], h * 2 + 1)
                act.wait_ge(s["x_added"], oi * NT + LEAD)
                for sign, dst in ((GATE, qd), (-GATE, kd)):
                    act.activation(dst[:, :, 0:SMP], ee[:, :, 0:SMP], ACT.Exp, scale=sign)
                    last = act.activation(dst[:, :, SMP:NTOK], bb[:, :, SMP:NTOK], ACT.Exp, scale=sign)
                last.then_inc(s["exp_done"], 1)
                split(r + 2, 0)
                for n in range(2):
                    level_exp(n)
                act.drain()
                for kt in range(KH):
                    act.activation(ee[:, kt, 0:SMP], bb[:, kt, 0:SMP], ACT.Exp, scale=-GATE, bias=bend[:, kt:kt + 1])
                act.activation(ee[:, :, SMP:NTOK], ee[:, :, SMP:NTOK], ACT.Exp, scale=-GATE)
                act.activation(eb, bb[:, :, SMP:NTOK].rearrange("p k (b l) -> p k b l", l=LS)[:, :, :, LS - 1],
                               ACT.Exp, scale=GATE).then_inc(s["exp_done"], 1)
                for t in range(NT):
                    act.wait_ge(s["qkT_full"], h * NT + (B_HEADS * NT + t + 1))
                    v = T[t % 2][:, :].rearrange("p (q n) -> p q n", q=4)
                    act.activation(qkTc[:, 0:KH, P * t:P * t + P], v[:, 0:KH, :], ACT.Copy, scale=DK ** -0.5)
                    act.activation(qkTc[:, KH:2 * KH, P * t:P * t + P], v[:, KH:2 * KH, :], ACT.Copy)\
                       .then_inc(s["qkT_done"], 1)
                    if t < 2:
                        split(r + 2, 1 + t)
                split(r + 2, 3)
                split(r + 3, 0)
                act.wait_ge(s["dif_done"], h * 2 + 2)
                level_exp(2)
                split(r + 3, 1)
                act.wait_ge(s["kt_full"], h * 2 + 1)
                act.activation(ktok[:, 0:2, :], T[0][:, :].rearrange("p (t d) -> p t d", t=2), ACT.Copy)\
                   .then_inc(s["kt_done"], 1)
                act.wait_ge(s["kt_full"], h * 2 + 2)
                act.activation(ktok[:, 2, :], T[1][:, 0:DK], ACT.Copy, scale=parity[:, 0:1])
                act.activation(koc, T[1][:, 0:DK], ACT.Copy, scale=parity[:, 1:2]).then_inc(s["kt_done"], 1)
                split(r + 3, 2)
                split(r + 3, 3)
                for t in range(NT):
                    acc_ready(act, t, ai + 1, r + 3)
                    act.activation(vc[:, t, :], acc[:, t, :], ACT.Copy).then_inc(acc_out[t], 1)
                split(r + 4, 0)
                for kt in range(KH):
                    act.wait_ge(s["pst_full"], h * KH + (B_HEADS + kt + 1))
                    act.activation(pstc[:, kt, :], T[kt][:, :], ACT.Copy).then_inc(s["pst_done"], 1)
                for j in range(1, NSLOT):
                    split(r + 4, j)
                splits(r + 5)
                for t in range(NT):
                    acc_ready(act, t, ai + 2, r + 5)
                    if t == 0:
                        act.wait_ge(s["y_done"], h * NT + Z_GL + LEAD)
                    act.activation(wc[t], acc[:, t, :], ACT.Tanh, scale=0.5).then_inc(s["z_tanh"], 1)

            def level_exp(n):
                w = 64 << n
                v = lev[n % 2].rearrange("p k (n w) -> p k n w", w=w)
                for kt in range(KH):
                    act.activation(v[:, kt, :, 0:w // 2], v[:, kt, :, 0:w // 2], ACT.Exp, scale=-GATE)
                    last = act.activation(v[:, kt, :, w // 2:w], v[:, kt, :, w // 2:w], ACT.Exp, scale=GATE)
                last.then_inc(s["exp_done"], 1)

            walk(act, dict(start=start, modulation=modulation, gmlp=gmlp, ret_setup=nothing, ret=ret,
                           gla_setup=gla_setup, gla=gla, out=out, finish=nothing))

        @block.vector
        def _(dve):
            def split(r, j):
                jj, rr = (j + AHEAD) % NSLOT, r + (j + AHEAD) // NSLOT
                dve.wait_ge(s["hi_ready"], 4 * rr + (jj + 1))
                dve.tensor_tensor(wlo[jj][:, :, :], raw[jj][:, :, :], whi[jj][:, :, :].bitcast(F32),
                                  ALU.subtract).then_inc(s["lo_ready"], 1)

            def splits(r):
                for j in range(NSLOT):
                    split(r, j)

            def start():
                lead(dve, [s["sel_done"], s["va_done"], s["mix_done"], s["sT_done"], s["o_done"], *acc_out])
                dve.wait_ge(s["zero_done"], 1)
                dve.tensor_copy(cT[:, :, :], zero.rearrange("p (a b) -> p a b", a=1).to_broadcast([P, KT, CROW]))
                dve.wait_ge(s["th_done"], 1)
                dve.scalar_tensor_tensor(out=cTf, in0=cth, scalar=1.0,
                                         in1=SC[:, 0:KT * NC9].rearrange("p (k c) -> p k c", k=KT),
                                         op0=ALU.add, op1=ALU.mult)
                dve.drain()
                dve.tensor_scalar(cT[:, :, 0:NC9], cTf, 0.5, None, ALU.mult)
                dve.drain()
                dve.scalar_tensor_tensor(out=cT[:, :, LOROW:LOROW + NC9], in0=cTf, scalar=0.5,
                                         in1=cT[:, :, 0:NC9].bitcast(F32), op0=ALU.mult,
                                         op1=ALU.subtract).then_inc(s["cT_done"], 1)
                for j in range(AHEAD):
                    dve.wait_ge(s["hi_ready"], j + 1)
                    dve.tensor_tensor(wlo[j][:, :, :], raw[j][:, :, :], whi[j][:, :, :].bitcast(F32),
                                      ALU.subtract).then_inc(s["lo_ready"], 1)

            def x_stats(q):
                for t in range(NT):
                    dve.bn_stats(stats[:, t, bass.ds(q, 1), :].rearrange("p o c -> p (o c)"),
                                 x[:, t, bass.ds(q * W, W)])

            def norm(pieces, src, n, scale=None):
                aggregate(pieces, src)
                dve.tensor_tensor(sq, mean_var[:, :, 0], mean_var[:, :, 0], ALU.mult)
                dve.drain()
                dve.tensor_tensor(ms, sq, mean_var[:, :, 1], ALU.add)
                dve.drain()
                if scale is not None:
                    dve.tensor_tensor(ms, ms, scale, ALU.mult)
                    dve.drain()
                dve.tensor_scalar(ms, ms, EPS, None, ALU.add).then_inc(s["ms_done"], 1)
                dve.wait_ge(s["rstd_done"], n + 1)

            def aggregate(pieces, src):
                if src is not None:
                    for t in range(NT):
                        for q in range(pieces):
                            dve.bn_stats(stats[:, t, q, :], src(t, q))
                dve.drain()
                for t in range(NT):
                    dve.bn_aggr(small[:, 2 * t:2 * t + 2], stats[:, t, 0:pieces, :])
                dve.drain()

            def modulation(layer):
                def layer_norm():
                    if layer == 0:
                        dve.wait_ge(s["ws_in"], 16 * (1 + NB))
                        dve.memset(ws_nat[0:64, :, 64:P], 0.0).then_inc(s["ws_masked"], 1)
                        dve.wait_ge(s["bs_in"], 16 * (1 + NB))
                        dve.drain()
                        norm(4, None, 0)
                    else:
                        dve.wait_ge(s["x_added"], NT * O_GL + LEAD)
                        x_stats(3)
                        norm(4, None, 1 + A_HEADS + B_HEADS)
                        dve.wait_ge(s["lrw_hi"], 1)
                        dve.tensor_tensor(wlr[1], wlr_raw, wlr[0].bitcast(F32), ALU.subtract)\
                           .then_inc(s["lrw_done"], 1)
                    dve.wait_ge(s["ident_done"], 1)
                    for t in range(NT):
                        last = dve.tensor_scalar(diag[:, t, :], ident[:, :], rstd[:, t:t + 1], None, ALU.mult)
                    last.then_inc(s["diag_done"], 1)

                def selected(mh, q):
                    dve.wait_ge(s["sel_full"], mh * 2 + (12 * layer + q + 1) + LEAD)
                    dve.tensor_copy(modT[:, bass.ds(mh * 8 + 4 * q, 4), :],
                                    OB[q][:, 0:40].rearrange("p (c n) -> p c n", c=4)).then_inc(s["sel_done"], 1)

                def pair(mh, gate, before):
                    for q in range(2):
                        last = (before, 1) if q == 0 else (mh, 0)
                        for g in range(2 * NSLOT):
                            split(mh * 4 + (R_MOD[layer] + 2 * q + g // NSLOT), g % NSLOT)
                            if g == 3 and last[0] is not None and not (gate if q else gate and mh == 5):
                                selected(*last)
                            if g == 3 and gate and mh == 4 and q == 0:
                                layer_norm()
                                dve.drain()
                                dve.scalar_tensor_tensor(out=modT[:, KT:2 * KT, 0:NC9], in0=modT[:, KT:2 * KT, 0:NC9],
                                                         scalar=1.0,
                                                         in1=modT[:, KT:2 * KT, NC9:10].to_broadcast([P, KT, NC9]),
                                                         op0=ALU.add, op1=ALU.mult).then_inc(s["modT_done"], 1)
                                dve.drain()
                            n = 2 * NSLOT * (2 * (mh - 4) + q) + g if gate else 0
                            if gate and x_block(n) is not None:
                                sample_block(x_block(n))
                    if not gate:
                        dve.wait_ge(s["x_in"], 32)
                        x_stats(mh)

                def per_stream(k):
                    return modT[:, k, 1:NC9].rearrange("p (b o) -> p b o", o=1).to_broadcast([P, NB, LS])

                def sample_block(k):
                    dve.wait_ge(s["h_prompt"], layer * KT + k + 1)
                    hs = hf[k % 2][:, SMP:NTOK].rearrange("p (b l) -> p b l", b=NB)
                    dve.tensor_tensor(hs, acc[:, k % 2, SMP:NTOK].rearrange("p (b l) -> p b l", b=NB),
                                      per_stream(KT + k), ALU.mult)
                    dve.drain()
                    dve.tensor_tensor(hs, hs, per_stream(k), ALU.add).then_inc(s["h_done"], 1)
                modulation_loops(dve, pair, layer)

            def turned(before, q0, wide=False):
                kind, h, yi, yb = before
                for q in (q0, q0 + 1):
                    src = turn_bank(q, wide)[:, 0:NTOK].rearrange("p (o n) -> p o n", o=1)
                    dve.wait_ge(s["yb_hi"], yi + (q + 1))
                    dve.scalar_tensor_tensor(out=yT[1][:, bass.ds(yb + q, 1), :],
                                             in0=src, scalar=0.5,
                                             in1=yT[0][:, bass.ds(yb + q, 1), :].bitcast(F32),
                                             op0=ALU.mult, op1=ALU.subtract).then_inc(s["yb_lo"], 1)

            def silu(z0, th, z):
                for t in range(NT):
                    dve.wait_ge(s["z_tanh"], z0 + (t + 1))
                    dve.scalar_tensor_tensor(out=th(t), in0=th(t), scalar=1.0, in1=z(t),
                                             op0=ALU.add, op1=ALU.mult).then_inc(acc_out[t], 1)

            def mod_selected(mh, q):
                dve.wait_ge(s["sel_full"], mh * 2 + (12 + q + 1) + LEAD)
                dve.tensor_copy(modT[:, bass.ds(mh * 8 + 4 * q, 4), :],
                                SC[:, 40 * q:40 * q + 40].rearrange("p (c n) -> p c n", c=4)).then_inc(s["sel_done"], 1)

            def gmlp(h, hh, r, ai, before):
                dve.wait_ge(s["wsT_done"], 2)
                dve.drain()
                at_least(dve, s["mix_full"], h * NT + LEAD)
                dve.tensor_copy(wsT, wsT_all[:, bass.ds(h, 1), :, :].rearrange("p o i t -> p (o i) t"))
                dve.tensor_copy(bs_cur, bsT[:, :, bass.ds(h, 1)].rearrange("p i o -> p (i o)"))\
                   .then_inc(s["wcur_done"], 1)
                splits(r)
                splits(r + 1)
                if before:
                    turned(before, 0)
                    turned(before, 2)
                splits(r + 2)
                splits(r + 3)
                for t in range(NT):
                    dve.wait_ge(acc_out[t], ai + 1 + LEAD)
                aggregate(1, lambda t, q: va[:, t, :])
                dve.tensor_scalar(ms, mean_var[:, :, 1], EPS, None, ALU.add).then_inc(s["ms_done"], 1)
                dve.wait_ge(s["rstd_done"], h + 2)
                for t in range(NT):
                    dve.tensor_scalar(va[:, t, :], va[:, t, :], mean_var[:, t, 0:1], rstd[:, t:t + 1],
                                      ALU.subtract, ALU.mult)
                dve.drain()
                dve.wait_ge(s["ln_in"], h * 16 + 16)
                for t in range(NT):
                    dve.tensor_tensor(va[:, t, :], va[:, t, :], ln_g, ALU.mult).then_inc(s["va_done"], 1)
                splits(r + 4)
                mod_selected(h, 0)
                splits(r + 5)
                splits(r + 6)
                splits(r + 7)
                split(r + 8, 0)
                split(r + 8, 1)
                split(r + 8, 2)
                mod_selected(h, 1)
                split(r + 8, 3)
                for t in range(NT):
                    dve.wait_ge(s["mix_full"], h * NT + (t + 1) + LEAD)
                    dve.wait_ge(acc_out[t], ai + 2 + LEAD)
                    dve.scalar_tensor_tensor(out=ug[:, t, :], in0=(OB[0], OB[1], SC)[t][:, :],
                                             scalar=bs_cur[:, t // 2:t // 2 + 1], in1=ug[:, t, :],
                                             op0=ALU.add, op1=ALU.mult).then_inc(s["mix_done"], 1)
                splits(r + 9)
                silu(h * NT, lambda t: wz[:, t, :], lambda t: acc[:, t, :])

            def out(kind, pn, kb, r, ai, yi, oi, last, before):
                split(r, 0)
                if kind != "gm" and not (isinstance(pn, int) and pn == 0):
                    dve.drain()
                    dve.wait_ge(s["x_added"], oi * NT + LEAD)
                    apart(dve)
                    x_stats(pn - 1)
                if not last:
                    if kind == "rt" and before:
                        ret_update(before, 0)
                        ret_update(before, 1)
                    split(r, 1)
                    if kind == "rt" and before:
                        ret_update(before, 2)
                        ret_update(before, 3)
                        ret_norm(before)
                    if kind != "rt" and before:
                        turned(before, 0, True)
                        turned(before, 2, True)
                    split(r, 2)
                    if kind == "rt" and before:
                        turned(before, 0, True)
                    split(r, 3)
                dve.wait_ge(s["g_in"], oi * 32 + 32)
                for t in range(NT):
                    acc_ready(dve, t, ai, r)
                    at_least(dve, s["x_added"], oi * NT + (t - 2) + LEAD)
                    dve.tensor_tensor(out_tmp[kind][:, t, :], acc[:, t, :], out_g[kind][:, t // 2, :], ALU.mult)\
                       .then_inc(acc_out[t], 1)

            def ret_update(before, c):
                for i in range(2):
                    dve.wait_ge(s["up_full"], before[1] * (2 * CH_RT) + (2 * c + i + 1))
                    half = state[c][:, W * i:W * i + W]
                    dve.scalar_tensor_tensor(out=half, in0=half, scalar=hc[:, HC_S:HC_S + 1], in1=T[i][:, :],
                                             op0=ALU.mult, op1=ALU.add).then_inc(s["up_done"], 1)

            def ret_norm(before):
                h = before[1]
                dve.wait_ge(s["o_full"], h * 2 + 2)

                def o_tile(t):
                    return OB[0][:, DVB * t:DVB * t + DVB] if t < 2 else OB[1][:, 0:DVB]
                norm(1, lambda t, q: o_tile(t), h + (1 + A_HEADS), hc[:, HC_Q2:HC_Q2 + NT])
                dve.tensor_tensor(fac, rstd, hc[:, HC_Q:HC_Q + NT], ALU.mult)
                dve.drain()
                for t in range(NT):
                    dve.scalar_tensor_tensor(out=onb[:, t, :], in0=o_tile(t), scalar=fac[:, t:t + 1], in1=ret_g,
                                             op0=ALU.mult, op1=ALU.mult).then_inc(s["o_done"], 1)

            def ret_setup():
                dve.wait_ge(s["rt_const"], 16 * 5)
                dve.tensor_copy(mask_u, mask01)

            def ret(h, r, ai, oi, before):
                split(r, 0)
                for c in range(CH_RT):
                    split(r + (c + 1) // NSLOT, (c + 1) % NSLOT)
                    if before:
                        ret_update(before, c)
                if before:
                    ret_norm(before)
                split(r + 1, 1)
                split(r + 1, 2)
                if before:
                    turned(before, 0)
                split(r + 1, 3)
                dve.drain()
                dve.tensor_copy(hc, hc_all[:, bass.ds(h, 1), :].rearrange("p o c -> p (o c)"))
                for t in range(NT):
                    dve.drain()
                    dve.wait_ge(acc_out[t], ai + 1 + LEAD)
                    v = qkr[:, t, :].rearrange("p (q e n) -> p q e n", q=2, e=2)
                    sv = swp.rearrange("p (q e n) -> p q e n", q=2, e=2)
                    sn_t = sn[:, t:t + 1, :].to_broadcast([P, 2, P])
                    dve.tensor_tensor(sv[:, :, 0, :], v[:, :, 1, :], sn_t, ALU.mult)
                    dve.tensor_tensor(sv[:, :, 1, :], v[:, :, 0, :], sn_t, ALU.mult)
                    dve.drain()
                    v4 = qkr[:, t, :].rearrange("p (q n) -> p q n", q=4)
                    dve.tensor_tensor(v4, v4, cs[:, t:t + 1, :].to_broadcast([P, 4, P]), ALU.mult)
                    dve.drain()
                    o = qkr[:, t, :].rearrange("p (q e n) -> p q e n", q=2, e=2)
                    dve.tensor_tensor(o[:, :, 0, :], o[:, :, 0, :], sv[:, :, 0, :], ALU.subtract)
                    dve.tensor_tensor(o[:, :, 1, :], o[:, :, 1, :], sv[:, :, 1, :], ALU.add).then_inc(s["rot_done"], 1)
                splits(r + 2)
                dve.wait_ge(s["qkT_full"], h * NT + NT)
                k2 = qkr[:, 2, DK:2 * DK]
                dve.tensor_scalar(kob, k2, hc[:, HC_KO:HC_KO + 1], None, ALU.mult)
                for t in range(2):
                    kt_ = qkr[:, t, DK:2 * DK]
                    dve.tensor_scalar(kt_, kt_, hc[:, HC_K + t:HC_K + t + 1], None, ALU.mult)
                dve.drain()
                dve.tensor_scalar(k2, k2, hc[:, HC_KE:HC_KE + 1], None, ALU.mult).then_inc(s["kd_done"], 1)
                splits(r + 3)
                dve.wait_ge(s["sc_full"], h + 1)
                for n, (c0, c1) in enumerate(((0, 256), (256, 384), (384, 512))):
                    last = dve.scalar_tensor_tensor(out=sTb[:, c0:c1], in0=SC[:, c0:c1],
                                                    scalar=hc[:, HC_PW + n:HC_PW + n + 1], in1=mask01[:, c0:c1],
                                                    op0=ALU.mult, op1=ALU.mult)
                last.then_inc(s["sT_done"], 1)
                silu(h * NT + Z_RT, lambda t: wb[:, t, :], lambda t: acc[:, t, DVB:W])

            def gla_setup():
                dve.drain()
                dve.wait_ge(s["sel_full"], 24 + LEAD)
                dve.memset(sTc, 0.0)
                dve.wait_ge(s["gl_const"], 48)
                dve.wait_ge(s["pst_out"], 16 * B_HEADS)

            def level_diff(n):
                w = 64 << n
                v = lev[n % 2].rearrange("p k (n w) -> p k n w", w=w)
                b = bb[:, :, 0:SMP].rearrange("p k (n w) -> p k n w", w=w)
                for kt in range(KH):
                    last = dve.tensor_tensor(v[:, kt], b[:, kt],
                                             b[:, kt, :, w // 2 - 1:w // 2].to_broadcast([P, SMP // w, w]),
                                             ALU.subtract)
                return last

            def level_mult(n):
                w = 64 << n
                v = lev[n % 2].rearrange("p k (n w) -> p k n w", w=w)
                q = qkTc[:, 0:KH, 0:SMP].rearrange("p k (n w) -> p k n w", w=w)
                k = qkTc[:, KH:2 * KH, 0:SMP].rearrange("p k (n w) -> p k n w", w=w)
                for kt in range(KH):
                    dve.tensor_tensor(v[:, kt, :, 0:w // 2], v[:, kt, :, 0:w // 2], k[:, kt, :, 0:w // 2], ALU.mult)
                    last = dve.tensor_tensor(v[:, kt, :, w // 2:w], v[:, kt, :, w // 2:w], q[:, kt, :, w // 2:w],
                                             ALU.mult)
                last.then_inc(s["dec_done"], 1)

            def gla(h, r, ai, oi, before):
                split(r, 0)
                split(r, 1)
                split(r, 2)
                if before:
                    turned(before, 0)
                split(r, 3)
                if before:
                    turned(before, 2)
                dve.wait_ge(s["gk_ln"], h + 1)
                for kt in range(KH):
                    dve.scalar_tensor_tensor(out=ee[:, kt, :], in0=OB[kt][:, 0:NTOK], scalar=0.0, in1=ee[:, kt, :],
                                             op0=ALU.min, op1=ALU.subtract).then_inc(s["gk_done"], 1)
                dve.drain()
                for kt in range(KH):
                    dve.tensor_tensor_scan(bb[:, kt, :], smask, ee[:, kt, :], 0.0, ALU.mult, ALU.add)
                dve.drain()
                dve.tensor_scalar(bend, bb[:, :, SMP - 1], GATE, None, ALU.mult)
                dve.wait_ge(s["pst_out"], h * 16 + 16 * B_HEADS)
                level_diff(0)
                level_diff(1)
                b32 = bb[:, :, 0:SMP].rearrange("p k (n w) -> p k n w", w=32)
                e32 = ee[:, :, 0:SMP].rearrange("p k (n w) -> p k n w", w=32)
                b16 = bb[:, :, SMP:NTOK].rearrange("p k (n w) -> p k n w", w=LS)
                e16 = ee[:, :, SMP:NTOK].rearrange("p k (n w) -> p k n w", w=LS)
                for kt in range(KH):
                    dve.tensor_tensor(e16[:, kt], b16[:, kt], b16[:, kt, :, LS - 1:LS].to_broadcast([P, NB, LS]),
                                      ALU.subtract)
                    last = dve.tensor_tensor(e32[:, kt], b32[:, kt], b32[:, kt, :, 15:16].to_broadcast([P, 8, 32]),
                                             ALU.subtract)
                last.then_inc(s["dif_done"], 1)
                splits(r + 1)
                split(r + 2, 0)
                split(r + 2, 1)
                dve.wait_ge(s["qkT_done"], h * NT + (B_HEADS + 1) * NT)
                dve.wait_ge(s["exp_done"], h * 5 + 4)
                dve.tensor_tensor(qd, qd, qkTc[:, 0:KH, :], ALU.mult)
                dve.tensor_tensor(kd, kd, qkTc[:, KH:2 * KH, :], ALU.mult).then_inc(s["dec_done"], 1)
                level_mult(0)
                level_mult(1)
                dve.tensor_tensor(ee, ee, qkTc[:, KH:2 * KH, :], ALU.mult).then_inc(s["dec_done"], 1)
                split(r + 2, 2)
                split(r + 2, 3)
                dve.wait_ge(s["lev_used"], h + 1)
                level_diff(2).then_inc(s["dif_done"], 1)
                split(r + 3, 0)
                dve.wait_ge(s["exp_done"], h * 5 + 5)
                level_mult(2)
                split(r + 3, 1)
                split(r + 3, 2)
                dve.wait_ge(s["sc_full"], h + (B_HEADS + 1))
                apart(dve)
                dve.copy_predicated(sTc, mask_u, SC[:, :]).then_inc(s["sT_done"], 1)
                split(r + 3, 3)
                for c in range(CH_GL):
                    split(r + 4 + c // NSLOT, c % NSLOT)
                    if c == CH_GL - 1:
                        silu(h * NT + Z_GL, lambda t: wc[t], lambda t: acc[:, t, :])
                    for i in range(2):
                        b = 2 * (c % 4) + i
                        dve.wait_ge(s["up_full"], h * (2 * CH_GL) + (2 * N_RT + 2 * c + i + 1))
                        half = state[c % NST][:, W * i:W * i + W]
                        dve.scalar_tensor_tensor(out=half, in0=half, scalar=eb[:, c // 4, b:b + 1], in1=T[i][:, :],
                                                 op0=ALU.mult, op1=ALU.add).then_inc(s["up_done"], 1)
                dve.wait_ge(s["o_full"], h * 2 + (2 * B_HEADS + 2))
                o_banks = (OB[0], OB[1], SC)
                norm(1, lambda t, q: o_banks[t][:, :], h + (2 + A_HEADS + B_HEADS))
                for t in range(NT):
                    dve.scalar_tensor_tensor(out=onc[:, t, :], in0=o_banks[t][:, :], scalar=rstd[:, t:t + 1],
                                             in1=gla_g, op0=ALU.mult, op1=ALU.mult).then_inc(s["o_done"], 1)

            def finish():
                dve.wait_ge(s["x_added"], NT * 32 + LEAD)
                x_stats(3)
                norm(4, None, 2 + A_HEADS + B_HEADS + C_HEADS)
                dve.wait_ge(s["fg_in"], 16)
                for t in range(NT):
                    dve.scalar_tensor_tensor(out=x[:, t, :], in0=x[:, t, :], scalar=rstd[:, t:t + 1],
                                             in1=work[:, 0:D], op0=ALU.mult, op1=ALU.mult).then_inc(s["final_done"], 1)

            walk(dve, dict(start=start, modulation=modulation, gmlp=gmlp, ret_setup=ret_setup, ret=ret,
                           gla_setup=gla_setup, gla=gla, out=out, finish=finish))

        @block.tensor
        def _(pe):
            def mm(out, lhsT, rhs, start=True, stop=True):
                return pe.matmul(out, lhsT, rhs, start=start, stop=stop, skip_group_check=True)

            def granule(r, j, lhs, k0, first, last, ai):
                pe.wait_ge(s["lo_ready"], 4 * r + (j + 1))
                for t in range(NT):
                    if first:
                        at_least(pe, acc_out[t], ai + LEAD)
                    for k in range(GK):
                        a_hi, a_lo = (part[:, k0 + k, P * t:P * t + P] for part in lhs)
                        mm(acc[:, t, :], a_hi, whi[j][:, k, :], first and k == 0, False)
                        mm(acc[:, t, :], a_hi, wlo[j][:, k, :], False, False)
                        ins = mm(acc[:, t, :], a_lo, whi[j][:, k, :], False, last and k == GK - 1)
                    if last and t < 2:
                        ins.then_inc(s["acc_full"], 1)
                ins.then_inc(s["w_used"], 1)

            def project(r, ai, steps={}):
                for g in range(2 * NSLOT):
                    granule(r + g // NSLOT, g % NSLOT, hT, GK * g, g == 0, g == 2 * NSLOT - 1, ai)
                    if g in steps:
                        steps[g]()

            def start():
                lead(pe, [s["w_used"], s["sel_full"], s["mix_full"], s["gk_full"]])
                pe.wait_ge(s["ident_done"], 1)
                pe.wait_ge(s["c_in"], 32)
                for k in range(KT):
                    ins = pe.transpose(SC[:, NC9 * k:NC9 * k + NC9], crow[0:NC9, P * k:P * k + P], ident[0:NC9, 0:NC9])
                ins.then_inc(s["cT_full"], 1)
                pe.wait_ge(s["const_in"], 16)

            def modulation(layer):
                pe.wait_ge(s["cT_done"], 1)

                def select(mh, q, gate):
                    pe.wait_ge(s["modsb_done"], mh * 2 + (12 * layer + q + 1) + LEAD)
                    pe.wait_ge(rows_in[q], mh * 32 + (6 * layer + 1) * 32)
                    at_least(pe, s["sel_done"], mh * 2 + (12 * layer + q - 1) + LEAD)
                    if gate:
                        ins = mm(OB[q][0:NC9, :], sel[0:NROW, 0:NC9], modsb[q][0:NROW, :])
                    else:
                        for c in range(4):
                            ins = mm(OB[q][:, 10 * c:10 * c + 10], modsb[q][0:NROW, P * c:P * c + P], sel[0:NROW, :])
                    ins.then_inc(s["sel_full"], 1)

                def pair(mh, gate, before):
                    for q in range(2):
                        for g in range(2 * NSLOT):
                            r, j = mh * 4 + (R_MOD[layer] + 2 * q + g // NSLOT), g % NSLOT
                            pe.wait_ge(s["lo_ready"], 4 * r + (j + 1))
                            if g == 0:
                                at_least(pe, s["modsb_done"], mh * 2 + (12 * layer + q - 1) + LEAD)
                            for k in range(GK):
                                kk = GK * g + k
                                mm(T[q][0:CROW, :], cT[:, kk, :], whi[j][:, k, :], kk == 0, False)
                                ins = mm(T[q][0:CROW, :], cT[:, kk, :], wlo[j][:, k, :], False, kk == KT - 1)
                            ins.then_inc(s["w_used"], 1)
                            if g == 2 and q == 0 and before is not None:
                                select(before, 1, gate and mh == 5)
                            if g == 2 and q == 1:
                                select(mh, 0, gate)
                            if not gate:
                                continue
                            n = 2 * NSLOT * (2 * (mh - 4) + q) + g
                            if layer == 0 and n in (8, 10):
                                pe.wait_ge(s["ws_masked"], 1)
                                if n == 10:
                                    pe.wait_ge(s["wsT_done"], 1)
                                for h in range(A_HEADS):
                                    ins = pe.transpose(acc[:, 2, P * h:P * h + P], (ws_nat, ws_diag)[n // 2 - 4][:, h, :],
                                                       ident[:, :])
                                ins.then_inc(s["wsT_full"], 1)
                            if x_block(n) is not None:
                                turn_x(x_block(n))

                def turn_x(k):
                    pe.wait_ge(s["diag_done"], layer + 1)
                    at_least(pe, s["h_done"], layer * KT + k - 1)
                    for t in range(NT):
                        ins = mm(acc[:, k % 2, P * t:P * t + P], x[:, t, P * k:P * k + P], diag[:, t, :])
                    ins.then_inc(s["xT_full"], 1)
                modulation_loops(pe, pair, layer)
                select(5, 1, True)
                pe.wait_ge(s["hT_done"], KT * layer + KT // 2)
                pe.wait_ge(s["h_done"], KT * (layer + 1))

            y_of = {"gm": (ug, NT), "rt": (onb, Z_RT + NT), "gl": (onc, Z_GL + NT)}

            def turn_out(before, q0, wide=False):
                kind, h, yi, yb = before
                y, z0 = y_of[kind]
                if q0 and not wide:
                    pe.wait_ge(s["yb_lo"], yi + q0)
                if q0 == 0:
                    pe.wait_ge(s["y_done"], h * NT + (z0 + LEAD))
                    if kind == "rt":
                        pe.wait_ge(s["up_done"], h * (2 * CH_RT) + 2 * CH_RT)
                    if kind == "gl":
                        pe.wait_ge(s["up_done"], h * (2 * CH_GL) + (2 * N_RT + 2 * CH_GL))
                for q in (q0, q0 + 1):
                    for t in range(NT):
                        ins = pe.transpose(turn_bank(q, wide)[:, P * t:P * t + P], y[:, t, P * q:P * q + P], ident[:, :])
                    ins.then_inc(s["yb_full"], 1)

            def turned(before):
                kind, h, yi, yb = before
                pe.wait_ge(s["yb_lo"], yi + (2 if kind == "rt" else 4))

            def end_steps(before, at):
                if not before:
                    return {}
                return {at: lambda: turn_out(before, 0), at + 1: lambda: turn_out(before, 2),
                        at + 2: lambda: turned(before)}

            def gmlp(h, hh, r, ai, before):
                def both(q, steps):
                    for g in range(2 * NSLOT):
                        rr, j = r + (4 * q + g // 2), 2 * (g % 2)
                        if q == 0 and g == NSLOT:
                            pe.wait_ge(s["hT_done"], KT)
                        granule(rr, j, hT, GK * g, g == 0, g == 2 * NSLOT - 1, ai + q)
                        pe.wait_ge(s["lo_ready"], 4 * rr + (j + 2))
                        if g == 0 and q == 0:
                            pe.wait_ge(s["mix_done"], h * NT + LEAD)
                            pe.wait_ge(s["sel_done"], h * 2 + (12 + LEAD))
                        for k in range(GK):
                            kk = GK * g + k
                            mm(OB[q][0:CROW, :], cT[:, kk, :], whi[j + 1][:, k, :], kk == 0, False)
                            ins = mm(OB[q][0:CROW, :], cT[:, kk, :], wlo[j + 1][:, k, :], False, kk == KT - 1)
                        ins.then_inc(s["w_used"], 1)
                        if g in steps:
                            steps[g]()

                def select(q):
                    pe.wait_ge(s["modsb_done"], h * 2 + (12 + q + 1) + LEAD)
                    pe.wait_ge(rows_in[q], h * 32 + 7 * 32)
                    for c in range(4):
                        ins = mm(SC[:, 40 * q + 10 * c:40 * q + 10 * c + 10], modsb[q][0:NROW, P * c:P * c + P],
                                 sel[0:NROW, :])
                    ins.then_inc(s["sel_full"], 1)
                both(0, end_steps(before, 2))
                both(1, {0: lambda: select(0)})

                def mix():
                    pe.wait_ge(s["va_done"], h * NT + NT + LEAD)
                    pe.wait_ge(s["sel_done"], h * 2 + 14 + LEAD)
                    pe.wait_ge(s["wcur_done"], h + 1)
                    at_least(pe, s["mix_done"], h * NT + LEAD)
                    for t in range(NT):
                        mm((OB[0], OB[1], SC)[t][:, :], wsT[:, t // 2, :], va[:, t, :]).then_inc(s["mix_full"], 1)
                project(r + 8, ai + 2, {0: lambda: select(1), 3: mix})

            def out(kind, pn, kb, r, ai, yi, oi, last, before):
                for g in range(NSLOT):
                    granule(r, g, yT, GK * g, g == 0, g == NSLOT - 1, ai)
                    if before and kind == "rt":
                        if g == 0:
                            ret_prompt(before)
                            ret_piece(before, 0)
                            ret_piece(before, 1)
                        if g == 1:
                            ret_piece(before, 2)
                            ret_piece(before, 3)
                        if g == 2:
                            turn_out(before, 0, True)
                            turned(before)
                    elif before:
                        if g == 1:
                            turn_out(before, 0, True)
                            turn_out(before, 2, True)
                            pe.wait_ge(s["yb_lo"], before[2] + 2)
                        if g == 2:
                            turned(before)

            def ret_setup():
                pe.wait_ge(s["mix_done"], NT * A_HEADS + LEAD)

            def ret_prompt(before):
                h = before[1]
                pe.wait_ge(s["sT_done"], h + 1 + LEAD)
                pe.wait_ge(s["v_done"], h * NT + NT)
                pe.wait_ge(s["o_done"], h * NT + LEAD)
                mm(OB[0][:, 0:DVB], sTb[:, 0:P], vb[:, 0, :])
                mm(OB[0][:, DVB:W], sTb[:, P:2 * P], vb[:, 0, :], True, False)
                mm(OB[0][:, DVB:W], sTb[:, 2 * P:3 * P], vb[:, 1, :], False, True).then_inc(s["o_full"], 1)
                pe.wait_ge(s["kd_done"], h + 1)
                for kt in range(KH):
                    for t in range(2):
                        ins = mm(T[1][:, DVB * kt:DVB * kt + DVB], qkr[:, t, DK + P * kt:DK + P * kt + P],
                                 vb[:, t, :], t == 0, t == 1)
                ins.then_inc(s["pst_full"], 1)
                mm(OB[1][:, 0:DVB], sTb[:, 3 * P:4 * P], vb[:, 2, :], True, False)
                pe.wait_ge(s["qm_done"], h + 1)

            def ret_piece(before, c):
                h, kt = before[1], c // 2
                pe.wait_ge(st_in[c], h * 16 + 16)
                for i in range(4):
                    b = 4 * (c % 2) + i
                    g0 = 32 * (b // 2)
                    ins = mm(OB[1][g0:g0 + 32, 0:DVB], qmask[:, kt, b, :], state[c][:, DVB * i:DVB * i + DVB],
                             False, c >= 2)
                if c == CH_RT - 1:
                    ins.then_inc(s["o_full"], 1)
                for i in range(2):
                    g0 = 32 * (2 * (c % 2) + i)
                    if c:
                        pe.wait_ge(s["up_done"], h * (2 * CH_RT) + (2 * c - 1 + i))
                    elif i:
                        pe.wait_ge(s["pst_done"], h + 1)
                    for e, k_tok in enumerate((qkr[:, 2, DK:2 * DK], kob)):
                        ins = mm(T[i][:, DVB * e:DVB * e + DVB], k_tok[g0:g0 + 32, P * kt:P * kt + P],
                                 vb[g0:g0 + 32, 2, :])
                    ins.then_inc(s["up_full"], 1)

            def ret(h, r, ai, oi, before):
                if before:
                    project(r, ai, {0: lambda: ret_prompt(before), 1: lambda: ret_piece(before, 0),
                                    2: lambda: ret_piece(before, 1), 3: lambda: ret_piece(before, 2),
                                    4: lambda: ret_piece(before, 3), 6: lambda: turn_out(before, 0),
                                    7: lambda: turned(before)})
                else:
                    project(r, ai)

                def turn(t):
                    pe.wait_ge(s["rot_done"], h * NT + (t + 1))
                    if t == 2:
                        pe.wait_ge(s["qkT_done"], h * NT + 1)
                    for q in range(4):
                        ins = pe.transpose(T[t % 2][:, P * q:P * q + P], qkr[:, t, P * q:P * q + P], ident[:, :])
                    ins.then_inc(s["qkT_full"], 1)

                def first_turns():
                    turn(0)
                    turn(1)

                def scores():
                    pe.wait_ge(s["qkT_done"], h * NT + NT)
                    at_least(pe, s["sT_done"], h + LEAD)
                    for k0, q0, n, c0 in ((0, 0, 256, 0), (128, 128, 128, 256), (256, 256, 128, 384)):
                        for kt in range(KH):
                            ins = mm(SC[:, c0:c0 + n], qkT[:, KH + kt, k0:k0 + P], qkT[:, kt, q0:q0 + n],
                                     kt == 0, kt == KH - 1)
                    ins.then_inc(s["sc_full"], 1)
                project(r + 2, ai + 1, {1: first_turns, 2: lambda: turn(2), 5: scores})

            def gla_setup():
                pe.wait_ge(s["lrw_done"], 1)
                pe.wait_ge(s["o_done"], NT * B_HEADS + LEAD)
                for k in range(KT):
                    if k == KT // 2:
                        pe.wait_ge(s["hT_done"], 2 * KT)
                    for n, (hp, wp) in enumerate(((0, 0), (0, 1), (1, 0))):
                        ins = mm(SC[0:RANK, 0:NTOK], wlr[wp][:, k, :], hT[hp][:, k, :],
                                 k == 0 and n == 0, k == KT - 1 and n == 2)
                ins.then_inc(s["lrT_full"], 1)
                pe.wait_ge(s["lrT_done"], 1)

            def gla(h, r, ai, oi, before):
                def gates():
                    pe.wait_ge(s["gkw_in"], h * 32 + 32)
                    pe.wait_ge(s["o_done"], h * NT + B_HEADS * NT + LEAD)
                    for kt in range(KH):
                        mm(OB[kt][:, 0:NTOK], gkw[0:RANK + 1, P * kt:P * kt + P], lrT[0:RANK + 1, :])\
                            .then_inc(s["gk_full"], 1)
                project(r, ai, {1: gates, **end_steps(before, 2)})

                def turn(t):
                    pe.wait_ge(acc_out[t], ai + 1 + LEAD)
                    if t == 2:
                        pe.wait_ge(s["qkT_done"], h * NT + (B_HEADS * NT + 1))
                    for q in range(4):
                        ins = pe.transpose(T[t % 2][:, P * q:P * q + P], vc[:, t, P * q:P * q + P], ident[:, :])
                    ins.then_inc(s["qkT_full"], 1)

                def first_turns():
                    turn(0)
                    turn(1)

                def block_scores(key, query, k0, k1, q0, q1, c0):
                    row = k0 % P
                    for kt in range(KH):
                        ins = mm(SC[row:row + k1 - k0, c0:c0 + q1 - q0], key[:, kt, k0:k1], query[:, kt, q0:q1],
                                 kt == 0, kt == KH - 1)
                    return ins

                def diagonal():
                    pe.wait_ge(s["dec_done"], h * 5 + 1)
                    for t in range(2):
                        for i in range(4):
                            k0 = P * t + 32 * i
                            block_scores(kd, qd, k0, k0 + 32, k0, k0 + 32, 256 * t + 32 * i)
                    block_scores(kd, qd, SMP, NTOK, SMP, NTOK, 384)

                def level(n):
                    w = 64 << n
                    v = lev[n % 2]
                    pe.wait_ge(s["dec_done"], h * 5 + (2, 3, 5)[n])
                    for m in range(SMP // w):
                        a0, mid = m * w, m * w + w // 2
                        t = a0 // P
                        c0 = mid if n == 2 else 256 * t + mid - P * t
                        ins = block_scores(v, v, a0, mid, mid, a0 + w, c0)
                    return ins

                def key_tails():
                    pe.wait_ge(s["dec_done"], h * 5 + 4)
                    pe.wait_ge(s["qkT_done"], h * NT + (B_HEADS + 1) * NT)
                    for t in range(NT):
                        for kt in range(KH):
                            c0 = DK * (t % 2) + P * kt
                            ins = pe.transpose(T[t // 2][:, c0:c0 + P], ee[:, kt, P * t:P * t + P], ident[:, :])
                        if t:
                            ins.then_inc(s["kt_full"], 1)

                project(r + 2, ai + 1, {
                    0: first_turns, 1: lambda: turn(2), 2: diagonal,
                    3: lambda: level(0).then_inc(s["lev_used"], 1), 4: lambda: level(1), 5: key_tails,
                    6: lambda: level(2).then_inc(s["sc_full"], 1)})

                def prompt():
                    for t in range(NT):
                        pe.wait_ge(acc_out[t], ai + 2 + LEAD)
                    pe.wait_ge(s["sT_done"], h + (B_HEADS + 1) + LEAD)
                    pe.wait_ge(s["gk_done"], h * KH + KH)
                    mm(OB[0][:, :], sTc[:, 0:P], vc[:, 0, :])
                    mm(OB[1][:, :], sTc[:, P:2 * P], vc[:, 0, :], True, False)
                    mm(OB[1][:, :], sTc[:, 2 * P:3 * P], vc[:, 1, :], False, True).then_inc(s["o_full"], 1)
                    pe.wait_ge(s["kt_done"], h * 2 + 2)
                    for kt in range(KH):
                        for t in range(2):
                            ins = mm(T[kt][:, :], ktok[:, t, P * kt:P * kt + P], vc[:, t, :], t == 0, t == 1)
                        ins.then_inc(s["pst_full"], 1)
                    mm(SC[:, :], sTc[:, 3 * P:4 * P], vc[:, 2, :], True, False)
                    pe.wait_ge(s["qm_done"], h + (B_HEADS + 1))

                def piece(c):
                    kt, g0 = c // 4, 32 * (c % 4)
                    pe.wait_ge(st_in[c % NST], h * 32 + 16 * (B_HEADS + c // NST + 1))
                    for i in range(2):
                        ins = mm(SC[g0:g0 + 32, :], qmask[:, kt, 2 * (c % 4) + i, :], state[c % NST][:, W * i:W * i + W],
                                 False, c >= 4)
                    if c == CH_GL - 1:
                        ins.then_inc(s["o_full"], 1)
                    for i, k_tok in enumerate((ktok[:, 2, :], koc)):
                        if c:
                            pe.wait_ge(s["up_done"], h * (2 * CH_GL) + (2 * N_RT + 2 * c - 1 + i))
                        else:
                            pe.wait_ge(s["pst_done"], h * KH + (B_HEADS + 1 + i))
                        mm(T[i][:, :], k_tok[g0:g0 + 32, P * kt:P * kt + P], vc[g0:g0 + 32, 2, :])\
                            .then_inc(s["up_full"], 1)

                def first_piece():
                    prompt()
                    piece(0)
                steps = {0: first_piece}
                for c in range(1, CH_GL):
                    steps[c] = lambda c=c: piece(c)
                project(r + 4, ai + 2, steps)

            walk(pe, dict(start=start, modulation=modulation, gmlp=gmlp, ret_setup=ret_setup, ret=ret,
                          gla_setup=gla_setup, gla=gla, out=out, finish=nothing))


def shape_constants():
    f32 = np.float32
    pos = np.concatenate([np.arange(256), np.tile(PAST + np.arange(LS), NB)]).astype(f32)
    freqs = f32(10000.0) ** (-np.arange(P, dtype=f32) / f32(P))
    ang = (pos[:, None] * freqs[None, :]).astype(f32)
    turned = [f(ang.astype(np.float64)).astype(f32).reshape(NT, P, P).transpose(1, 0, 2) for f in (np.cos, np.sin)]

    p = np.arange(P)
    i = p % LS
    causal = (p[None, :] >= p[:, None])
    same = (p[None, :] // LS) == (p[:, None] // LS)
    mask = np.concatenate([causal, np.ones((P, P), bool), causal, causal & same], axis=1)

    lg = np.log1p(-np.exp2(-5.0 - np.arange(B_HEADS)))
    hc = np.zeros((P, B_HEADS, 16), np.float64)
    for h in range(B_HEADS):
        g = lambda n: np.exp(lg[h] * n)
        sc = DK ** -0.5
        hc[:, h, HC_PW] = g(-(p + 1.0)) * sc
        hc[:, h, HC_PW + 1] = g(-(p + 129.0)) * sc
        hc[:, h, HC_PW + 2] = g(-(i + 1.0)) * sc
        for t, n in enumerate((p + 1.0, p + 129.0, i + 1.0)):
            hc[:, h, HC_Q + t] = g(n)
            hc[:, h, HC_Q2 + t] = g(2 * n)
        hc[:, h, HC_K] = g(255.0 - p) * sc
        hc[:, h, HC_K + 1] = g(127.0 - p) * sc
        even = (p // LS) % 2 == 0
        hc[:, h, HC_KE] = g(15.0 - i) * sc * even
        hc[:, h, HC_KO] = g(15.0 - i) * sc * ~even
        hc[:, h, HC_S] = g(16.0)
    sel = np.zeros((P, 10), f32)
    for c in range(NC9):
        sel[[c, LOROW + c, BROW], c] = 1.0
    sel[GROW, NC9] = 1.0
    scan = np.ones((P, NTOK), f32)
    scan[:, 0] = 0.0
    scan[:, 256::LS] = 0.0
    parity = np.stack([(p // LS) % 2 == 0, (p // LS) % 2 == 1], axis=1).astype(f32)
    return {"cos": turned[0], "sin": turned[1], "mask01": mask.astype(f32),
            "hc": hc.astype(f32), "sel": sel, "scan_mask": scan, "parity": parity}


_INS = ["x_prompt", "x_sample", "state_ret", "state_gla", "c_prompt", "c_sample", "norm_g", "w_mod", "b_mod", "w_in_e",
        "gmlp_ln_g", "gmlp_ws", "gmlp_bs", "ret_norm_g", "w_out_e", "w_in_o", "w_gk2", "b_gk", "gla_norm_g", "w_out_o",
        "final_g"]
_OUTS = [(1, 256, D), (NB, LS, D), (1, 1, B_HEADS, DK, DVB), (1, NB, B_HEADS, DK, DVB), (1, 1, C_HEADS, DK, DVC),
         (1, NB, C_HEADS, DK, DVC), (1, NB, LS, D)]


def kernel(**inputs):
    import concourse.bacc as bacc
    from concourse.bass_utils import run_bass_kernel_spmd

    nc = bacc.Bacc("TRN2", target_bir_lowering=False, num_devices=1)
    arrays = {}

    def dram_in(name, array):
        array = np.ascontiguousarray(array)
        arrays[name] = array
        return nc.dram_tensor(name, array.shape, mybir.dt.from_np(array.dtype), kind="ExternalInput").ap()

    args = {n: dram_in(f"in_{n}", inputs[n]) for n in _INS}
    consts = {n: dram_in(f"const_{n}", v) for n, v in shape_constants().items()}
    outs = [nc.dram_tensor(f"out_{i}", s, F32, kind="ExternalOutput").ap() for i, s in enumerate(_OUTS)]
    build(nc, args, consts, outs)
    r = run_bass_kernel_spmd(nc, [arrays], core_ids=[0])
    return tuple(r.results[0][f"out_{i}"] for i in range(len(_OUTS)))
```
